# Optimizing a Trainium2 kernel written in Bass

```python
import math
import jax
import jax.numpy as jnp
from jax import lax
import numpy as np

D_MODEL = 1024
BATCH = 1
SEQ = 512
DEPTH = 1
DEC_BATCH = 8
DEC_SEQ = 1
PAST_LEN = 4096
PAGE_SIZE = 128

MLSTM_HEADS = 4
MLSTM_WIDTH = D_MODEL
MLSTM_HEAD_DIM = MLSTM_WIDTH // MLSTM_HEADS
CHUNK = 128
S5_WIDTH = D_MODEL // 2
S5_GROUP = 16
S5_GROUPS = S5_WIDTH // S5_GROUP
S5_STATE = 64
D_FF = -(-(8 * D_MODEL) // (3 * 256)) * 256
P_TOTAL = 4 * MLSTM_WIDTH + 2 * MLSTM_HEADS + S5_WIDTH + 2 * D_MODEL
EPS = 1e-6

kernel_name = "mlstm_s5_gated_hybrid_step"

def rmsnorm(x, g):
    xf = x.astype(jnp.float32)
    return xf * lax.rsqrt(jnp.mean(xf * xf, axis=-1, keepdims=True) + EPS) * g.astype(jnp.float32)

def mlstm_chunk_step(carry, xs):
    C, n, m = carry
    q, k, v, ig, lf = xs
    L = q.shape[-2]
    causal = jnp.tril(jnp.ones((L, L), dtype=bool))
    b = jnp.cumsum(lf, axis=-1)
    dmat = b[..., :, None] - b[..., None, :] + ig[..., None, :]
    dmat = jnp.where(causal, dmat, -jnp.inf)
    inter = b + m[..., None]
    m_t = jnp.maximum(inter, jnp.max(dmat, axis=-1))
    w_inter = jnp.exp(inter - m_t)
    w_intra = jnp.exp(dmat - m_t[..., None])
    s = jnp.einsum('bhtd,bhsd->bhts', q, k) * w_intra
    num = w_inter[..., None] * jnp.einsum('bhtd,bhde->bhte', q, C) + jnp.einsum('bhts,bhse->bhte', s, v)
    den = w_inter * jnp.einsum('bhtd,bhd->bht', q, n) + jnp.sum(s, axis=-1)
    h = num / jnp.maximum(jnp.abs(den), jnp.exp(-m_t))[..., None]
    b_last = b[..., -1]
    g = b_last[..., None] - b + ig
    m_new = jnp.maximum(b_last + m, jnp.max(g, axis=-1))
    a = jnp.exp(b_last + m - m_new)
    wk = jnp.exp(g - m_new[..., None])
    C_new = a[..., None, None] * C + jnp.einsum('bhs,bhsd,bhse->bhde', wk, k, v)
    n_new = a[..., None] * n + jnp.einsum('bhs,bhsd->bhd', wk, k)
    return (C_new, n_new, m_new), h

def mlstm_mixer(q, k, v, ig, lf, C0, n0, m0):
    B, S = q.shape[0], q.shape[1]
    L = CHUNK if S % CHUNK == 0 else S
    nc = S // L

    def to_chunks(t):
        t = t.reshape((B, nc, L) + t.shape[2:])
        return jnp.moveaxis(t, (1, 2), (0, 3))

    xs = (to_chunks(q), to_chunks(k), to_chunks(v), to_chunks(ig), to_chunks(lf))
    (C, n, m), hs = lax.scan(mlstm_chunk_step, (C0, n0, m0), xs)
    hs = jnp.moveaxis(hs, (0, 3), (1, 2)).reshape(B, S, MLSTM_HEADS, MLSTM_HEAD_DIM)
    return hs, C, n, m

def s5_combine(e1, e2):
    a1r, a1i, b1r, b1i = e1
    a2r, a2i, b2r, b2i = e2
    return (a2r * a1r - a2i * a1i,
            a2r * a1i + a2i * a1r,
            a2r * b1r - a2i * b1i + b2r,
            a2r * b1i + a2i * b1r + b2i)

def s5_mixer(u, s0_re, s0_im, A_re, A_im, log_dt, B_re, B_im, C_re, C_im, D_skip):
    Bsz, S = u.shape[0], u.shape[1]
    ug = u.reshape(Bsz, S, S5_GROUPS, S5_GROUP)
    dt = jnp.exp(log_dt.astype(jnp.float32))[:, None]
    A_re = A_re.astype(jnp.float32)
    A_im = A_im.astype(jnp.float32)
    mag = jnp.exp(dt * A_re)
    abar_re = mag * jnp.cos(dt * A_im)
    abar_im = mag * jnp.sin(dt * A_im)
    den = A_re * A_re + A_im * A_im
    nr = abar_re - 1.0
    ni = abar_im
    f_re = (nr * A_re + ni * A_im) / den
    f_im = (ni * A_re - nr * A_im) / den
    B_re = B_re.astype(jnp.float32)
    B_im = B_im.astype(jnp.float32)
    bbar_re = f_re[..., None] * B_re - f_im[..., None] * B_im
    bbar_im = f_re[..., None] * B_im + f_im[..., None] * B_re
    bu_re = jnp.einsum('gpc,bsgc->bsgp', bbar_re, ug)
    bu_im = jnp.einsum('gpc,bsgc->bsgp', bbar_im, ug)
    bu_re = bu_re.at[:, 0].add(abar_re * s0_re - abar_im * s0_im)
    bu_im = bu_im.at[:, 0].add(abar_re * s0_im + abar_im * s0_re)
    a_re = jnp.broadcast_to(abar_re, bu_re.shape)
    a_im = jnp.broadcast_to(abar_im, bu_im.shape)
    _, _, s_re, s_im = lax.associative_scan(s5_combine, (a_re, a_im, bu_re, bu_im), axis=1)
    y = (jnp.einsum('gcp,bsgp->bsgc', C_re.astype(jnp.float32), s_re)
         - jnp.einsum('gcp,bsgp->bsgc', C_im.astype(jnp.float32), s_im))
    y = y.reshape(Bsz, S, S5_WIDTH) + D_skip.astype(jnp.float32) * u
    return y, s_re[:, -1], s_im[:, -1]

def hybrid_layer(x, state, p):
    C0, n0, m0, sr0, si0 = state
    (g_mix, w_in, b_in, g_hn, w_a, A_re, A_im, log_dt, B_re, B_im, C_re, C_im, D_skip,
     w_glu, b_glu, w_b, w_out, g_ffn, w_ff1, w_ff3, w_ff2) = p
    f32 = jnp.float32
    Bsz, S = x.shape[0], x.shape[1]
    H, DH, DA = MLSTM_HEADS, MLSTM_HEAD_DIM, MLSTM_WIDTH
    h = rmsnorm(x, g_mix)
    proj = h @ w_in.astype(f32) + b_in.astype(f32)
    offsets = [DA, 2 * DA, 3 * DA, 4 * DA, 4 * DA + H, 4 * DA + 2 * H, 4 * DA + 2 * H + S5_WIDTH]
    q, k, v, o, ig, fg, u, gl = jnp.split(proj, offsets, axis=-1)
    q = q.reshape(Bsz, S, H, DH)
    k = k.reshape(Bsz, S, H, DH) * (DH ** -0.5)
    v = v.reshape(Bsz, S, H, DH)
    lf = jax.nn.log_sigmoid(fg)
    hA, C, n, m = mlstm_mixer(q, k, v, ig, lf, C0.astype(f32), n0.astype(f32), m0.astype(f32))
    hA = hA * lax.rsqrt(jnp.mean(hA * hA, axis=-1, keepdims=True) + EPS)
    hA = hA.reshape(Bsz, S, DA) * g_hn.astype(f32)
    yA = (jax.nn.sigmoid(o) * hA) @ w_a.astype(f32)
    yS, sr, si = s5_mixer(u, sr0.astype(f32), si0.astype(f32), A_re, A_im, log_dt, B_re, B_im, C_re, C_im, D_skip)
    yS = jax.nn.gelu(yS)
    yS = yS * jax.nn.sigmoid(yS @ w_glu.astype(f32) + b_glu.astype(f32))
    yB = yS @ w_b.astype(f32)
    gA, gB = jnp.split(gl, 2, axis=-1)
    mix = (jax.nn.sigmoid(gA) * yA + jax.nn.sigmoid(gB) * yB) @ w_out.astype(f32)
    x = x.astype(f32) + mix
    hf = rmsnorm(x, g_ffn)
    x = x + (jax.nn.silu(hf @ w_ff1.astype(f32)) * (hf @ w_ff3.astype(f32))) @ w_ff2.astype(f32)
    return x, (C, n, m, sr, si)

def setup_inputs(seed: int = 0) -> dict:
    key = jax.random.key(seed)
    ks = jax.random.split(key, 32)
    f32 = jnp.float32

    def nrm(k, shape, scale):
        return jax.random.normal(k, shape, f32) * scale

    x_prompt = nrm(ks[0], (BATCH, SEQ, D_MODEL), 1.0)
    x_sample = nrm(ks[1], (DEC_BATCH, DEC_SEQ, D_MODEL), 1.0)
    state_mlstm_C = nrm(ks[2], (DEPTH, DEC_BATCH, MLSTM_HEADS, MLSTM_HEAD_DIM, MLSTM_HEAD_DIM), 0.05)
    state_mlstm_n = nrm(ks[3], (DEPTH, DEC_BATCH, MLSTM_HEADS, MLSTM_HEAD_DIM), 0.5)
    state_mlstm_m = nrm(ks[4], (DEPTH, DEC_BATCH, MLSTM_HEADS), 1.0)
    state_s5_re = nrm(ks[5], (DEPTH, DEC_BATCH, S5_GROUPS, S5_STATE), 0.5)
    state_s5_im = nrm(ks[6], (DEPTH, DEC_BATCH, S5_GROUPS, S5_STATE), 0.5)
    norm_mix_g = 1.0 + nrm(ks[7], (DEPTH, D_MODEL), 0.02)
    w_in = nrm(ks[8], (DEPTH, D_MODEL, P_TOTAL), D_MODEL ** -0.5)
    b_in = nrm(ks[9], (DEPTH, P_TOTAL), 0.02)
    f_off = 4 * MLSTM_WIDTH + MLSTM_HEADS
    b_in = b_in.at[:, f_off:f_off + MLSTM_HEADS].add(jnp.linspace(3.0, 6.0, MLSTM_HEADS, dtype=f32))
    mlstm_norm_g = 1.0 + nrm(ks[10], (DEPTH, MLSTM_WIDTH), 0.02)
    w_a = nrm(ks[11], (DEPTH, MLSTM_WIDTH, D_MODEL), MLSTM_WIDTH ** -0.5)
    n_idx = jnp.arange(S5_STATE, dtype=f32)
    s5_A_re = -0.5 + nrm(ks[12], (DEPTH, S5_GROUPS, S5_STATE), 0.01)
    s5_A_im = math.pi * n_idx + nrm(ks[13], (DEPTH, S5_GROUPS, S5_STATE), 0.01)
    s5_log_dt = jax.random.uniform(ks[14], (DEPTH, S5_GROUPS), f32, math.log(1e-3), math.log(1e-1))
    s5_B_re = nrm(ks[15], (DEPTH, S5_GROUPS, S5_STATE, S5_GROUP), (2 * S5_GROUP) ** -0.5)
    s5_B_im = nrm(ks[16], (DEPTH, S5_GROUPS, S5_STATE, S5_GROUP), (2 * S5_GROUP) ** -0.5)
    s5_C_re = nrm(ks[17], (DEPTH, S5_GROUPS, S5_GROUP, S5_STATE), S5_STATE ** -0.5)
    s5_C_im = nrm(ks[18], (DEPTH, S5_GROUPS, S5_GROUP, S5_STATE), S5_STATE ** -0.5)
    s5_D = nrm(ks[19], (DEPTH, S5_WIDTH), 0.5)
    w_glu = nrm(ks[20], (DEPTH, S5_WIDTH, S5_WIDTH), S5_WIDTH ** -0.5)
    b_glu = nrm(ks[21], (DEPTH, S5_WIDTH), 0.02)
    w_b = nrm(ks[22], (DEPTH, S5_WIDTH, D_MODEL), S5_WIDTH ** -0.5)
    w_out = nrm(ks[23], (DEPTH, D_MODEL, D_MODEL), D_MODEL ** -0.5)
    norm_ffn_g = 1.0 + nrm(ks[24], (DEPTH, D_MODEL), 0.02)
    w_ff1 = nrm(ks[25], (DEPTH, D_MODEL, D_FF), D_MODEL ** -0.5)
    w_ff3 = nrm(ks[26], (DEPTH, D_MODEL, D_FF), D_MODEL ** -0.5)
    w_ff2 = nrm(ks[27], (DEPTH, D_FF, D_MODEL), D_FF ** -0.5)
    norm_final_g = 1.0 + nrm(ks[28], (D_MODEL,), 0.02)
    return {
        "x_prompt": x_prompt, "x_sample": x_sample,
        "state_mlstm_C": state_mlstm_C, "state_mlstm_n": state_mlstm_n, "state_mlstm_m": state_mlstm_m,
        "state_s5_re": state_s5_re, "state_s5_im": state_s5_im,
        "norm_mix_g": norm_mix_g, "w_in": w_in, "b_in": b_in, "mlstm_norm_g": mlstm_norm_g, "w_a": w_a,
        "s5_A_re": s5_A_re, "s5_A_im": s5_A_im, "s5_log_dt": s5_log_dt,
        "s5_B_re": s5_B_re, "s5_B_im": s5_B_im, "s5_C_re": s5_C_re, "s5_C_im": s5_C_im, "s5_D": s5_D,
        "w_glu": w_glu, "b_glu": b_glu, "w_b": w_b, "w_out": w_out,
        "norm_ffn_g": norm_ffn_g, "w_ff1": w_ff1, "w_ff3": w_ff3, "w_ff2": w_ff2,
        "norm_final_g": norm_final_g,
    }

def reference(x_prompt, x_sample, state_mlstm_C, state_mlstm_n, state_mlstm_m, state_s5_re, state_s5_im,
              norm_mix_g, w_in, b_in, mlstm_norm_g, w_a, s5_A_re, s5_A_im, s5_log_dt,
              s5_B_re, s5_B_im, s5_C_re, s5_C_im, s5_D, w_glu, b_glu, w_b, w_out,
              norm_ffn_g, w_ff1, w_ff3, w_ff2, norm_final_g):
    f32 = jnp.float32
    Bp = x_prompt.shape[0]
    xp = x_prompt
    xs = x_sample
    pC, pn, pm, psr, psi = [], [], [], [], []
    sC, sn, sm, ssr, ssi = [], [], [], [], []
    for l in range(DEPTH):
        p = (norm_mix_g[l], w_in[l], b_in[l], mlstm_norm_g[l], w_a[l], s5_A_re[l], s5_A_im[l], s5_log_dt[l],
             s5_B_re[l], s5_B_im[l], s5_C_re[l], s5_C_im[l], s5_D[l], w_glu[l], b_glu[l], w_b[l], w_out[l],
             norm_ffn_g[l], w_ff1[l], w_ff3[l], w_ff2[l])
        zero_state = (jnp.zeros((Bp, MLSTM_HEADS, MLSTM_HEAD_DIM, MLSTM_HEAD_DIM), f32),
                      jnp.zeros((Bp, MLSTM_HEADS, MLSTM_HEAD_DIM), f32),
                      jnp.zeros((Bp, MLSTM_HEADS), f32),
                      jnp.zeros((Bp, S5_GROUPS, S5_STATE), f32),
                      jnp.zeros((Bp, S5_GROUPS, S5_STATE), f32))
        xp, st_p = hybrid_layer(xp, zero_state, p)
        past_state = (state_mlstm_C[l], state_mlstm_n[l], state_mlstm_m[l], state_s5_re[l], state_s5_im[l])
        xs, st_s = hybrid_layer(xs, past_state, p)
        pC.append(st_p[0]); pn.append(st_p[1]); pm.append(st_p[2]); psr.append(st_p[3]); psi.append(st_p[4])
        sC.append(st_s[0]); sn.append(st_s[1]); sm.append(st_s[2]); ssr.append(st_s[3]); ssi.append(st_s[4])
    y_prompt = rmsnorm(xp, norm_final_g).astype(x_prompt.dtype)
    y_sample = rmsnorm(xs, norm_final_g).astype(x_sample.dtype)
    new_C_prompt = jnp.stack(pC)
    new_n_prompt = jnp.stack(pn)
    new_m_prompt = jnp.stack(pm)
    new_s5_re_prompt = jnp.stack(psr)
    new_s5_im_prompt = jnp.stack(psi)
    new_C_sample = jnp.stack(sC)
    new_n_sample = jnp.stack(sn)
    new_m_sample = jnp.stack(sm)
    new_s5_re_sample = jnp.stack(ssr)
    new_s5_im_sample = jnp.stack(ssi)
    return (y_prompt, y_sample, new_C_prompt, new_n_prompt, new_m_prompt, new_s5_re_prompt, new_s5_im_prompt,
            new_C_sample, new_n_sample, new_m_sample, new_s5_re_sample, new_s5_im_sample)


_drawn_inputs = setup_inputs


def setup_inputs(seed=0):
    import zlib

    import numpy as np

    out = dict(_drawn_inputs(seed))
    spreads = {}
    factors = {'mlstm_norm_g': 8.0,
     's5_A_re': 16.86,
     'b_glu': 64.0,
     'norm_ffn_g': 4.003,
     'norm_final_g': 7.495,
     'w_glu': 2.92}
    for name, (base, spread) in spreads.items():
        noise = np.random.default_rng([zlib.crc32(name.encode()), seed]).standard_normal(out[name].shape)
        drawn = base * np.exp(spread * noise) if base else spread * noise
        out[name] = jnp.asarray(drawn.astype(out[name].dtype))
    for name, factor in factors.items():
        out[name] = (out[name] * factor).astype(out[name].dtype)
    return out
```

```python
from contextlib import ExitStack

import concourse.bass as bass
from concourse import mybir

F32 = mybir.dt.float32
F32R = mybir.dt.float32r
ALU = mybir.AluOpType
ACT = mybir.ActivationFunctionType

P = 128
D = 1024
KC = D // P
SEQ, NS = 512, 8
T = SEQ + NS
HALVES = ((0, 256), (256, 264))
H, DH = 4, 256
NE = DH // P
SC = SEQ // P
F_TILES = 22
L = 8
NB = SEQ // L
LEVELS = 6
PAIRS = 4
NCOL = 1 + NB + NS
U = 1024
RING = 3
EPS = 1e-6

N_GATES = 0
N_MIX = 1
PER_HEAD = 9
N_GLU = N_MIX + PER_HEAD * H
N_MERGE = N_GLU + 2
PER_MERGE = 4
N_OUT = N_MERGE + PER_MERGE * KC
N_FF = N_OUT + KC
N_DOWN = N_FF + 2 * F_TILES
DOWN_CUT = (0, 8, 15, 22)
N_UNITS = N_DOWN + 3 * KC
assert N_UNITS % RING == 0

HP = {}
_at = 0
for _name, _n in (("bias", 7), ("skip", 1), ("norm_g", 2), ("acol", SC), ("samp", 24),
                  ("scan_re", LEVELS * PAIRS), ("scan_im", 2 * LEVELS * PAIRS),
                  ("one_re", PAIRS), ("one_im", 2 * PAIRS), ("pick", 1)):
    HP[_name] = (_at, _at + _n)
    _at += _n
NHP = _at

SM = {}
_at = 0
for _name, _n in (("b_re", 1024), ("b_im", 1024), ("c_re", 512), ("c_im", 512),
                  ("s0", 256), ("n0", 64), ("ident", 128), ("m0", 8), ("b_gate", 2), ("hp", H * 10)):
    SM[_name] = (_at, _at + _n)
    _at += _n
NSM = _at


class At:

    def __init__(self, static, coef=0, i=None):
        self.static, self.coef, self.i = static, coef, i

    def plus(self, k):
        return At(self.static + k, self.coef, self.i)

    def val(self, scale=1, add=0):
        v = self.static * scale + add
        return v if self.i is None else self.coef * scale * self.i + v

    def slot(self):
        return self.static % RING

    def visits(self):
        return At(self.static // RING, self.coef // RING, self.i)


def steps(eng, count, per_step, body, first_unit, loops=None):
    loops = count // body if loops is None else loops
    with eng.Fori(0, loops) as i:
        for s in range(body):
            yield At(s, body, i), At(first_unit + per_step * s, per_step * body, i)
    for s in range(loops * body, count):
        yield At(s), At(first_unit + per_step * s)


class Order:

    def __init__(self, eng, sem):
        self.eng, self.sem, self.n, self.base, self.coef, self.i = eng, sem, 0, 0, 0, None

    def loop(self, i, coef):
        self.base, self.coef, self.i = self.n, coef, i

    def end(self, loops):
        assert self.n - self.base == self.coef, (self.n - self.base, self.coef)
        self.n, self.coef, self.i = self.base + self.coef * loops, 0, None

    def add(self, ins):
        ins.then_inc(self.sem, 1)
        self.n += 1

    def settle(self):
        self.eng.wait_ge(self.sem, self.n if self.i is None else self.coef * self.i + self.n)

    def do(self, ins):
        self.add(ins)
        self.settle()


def build(nc, wst, xt, small, apar, vbias, c0, y_o, cp_o, mp_o, s5p_o, cs_o, ns_o, ms_o, s5s_o):
    v_scr = nc.dram_tensor("v_scratch", (NS, DH), F32, kind="Internal").ap()
    ha_scr = nc.dram_tensor("heads_scratch", (P, KC, T), F32, kind="Internal").ap()

    ctx = ExitStack()
    with ctx:
        def sem(name):
            return ctx.enter_context(nc.semaphore(name))

        cursor = [-(-nc.sbuf_base // 64) * 64]

        def sb(name, shape, dt=F32, at=None, pad=0):
            n = 4
            for d in shape[1:]:
                n *= d
            if at is not None:
                assert at + n <= nc.sbuf_usable_end
                return nc.alloc_sbuf_tensor_at(name, shape, dt, offset=at)
            t = nc.alloc_sbuf_tensor_at(name, shape, dt, offset=cursor[0])
            cursor[0] += -(-(n + pad) // 64) * 64
            return t

        raw = [sb(f"raw{s}", [P, U]) for s in range(RING)]
        WH = [sb(f"w_high{s}", [P, U], F32R) for s in range(RING)]
        WL = [sb(f"w_low{s}", [P, U], F32R) for s in range(RING)]
        ones = sb("ones", [P, P])
        eps = sb("eps", [P, 1])
        half_pi = sb("half_pi", [P, 1])
        gb = sb("gains_biases", [P, 44])
        g_mix, g_ffn, g_fin, b_merge, b_glu = gb[:, 0:8], gb[:, 8:16], gb[:, 16:24], gb[:, 24:40], gb[:, 40:44]
        cur_b = sb("cur_b", [P, 2])
        junk_a = sb("unused_a", [P, 1])
        junk_p = sb("unused_p", [P, 16])
        junk_d = sb("unused_d", [P, 24])
        HH = sb("h_high", [P, KC, T], F32R)
        HL = sb("h_low", [P, KC, T], F32R)
        YS = sb("s5_out", [P, 4, T])

        at_small = cursor[0]
        sm = sb("small", [P, NSM])
        hp = sb("head_params", [P, H, NHP])
        cur = sb("cur_params", [P, NHP])
        a_pow = sb("abar_powers", [P, 2, 3, 272])
        CN = sb("c_im_negated", [P, 512])
        rows = sb("gate_rows", [2 * 32, 2, SEQ])
        BPs = sb("bbar_p", [P, 2, P // 4 * PAIRS])
        Kb = sb("conv_kernels", [P, L, P])
        at_ba = cursor[0]
        BA = sb("b_abar", [P, 2, L, P])
        CA = sb("c_abar", [P, 2, L + 1, P])
        assert cursor[0] - at_ba >= 2 * 4 * 4 * T
        S = sb("s5_state", [P, 2, PAIRS, NCOL])
        S1 = sb("s5_tmp1", [P, 2, PAIRS, NB])
        S2 = sb("s5_tmp2", [P, 2, PAIRS, NB])
        pt = [sb(f"pool_tmp{k}", [P, 4 * P]) for k in range(2)]
        uT = sb("uT", [P, T])
        s5p = sb("s5_prompt_out", [P, 2, 16])
        at_wt = cursor[0]
        Wt = sb("attn_weights", [P, SC, SEQ])
        KS = sb("k_scaled", [P, SC, DH])
        V = sb("V", [P, SC, DH + 1], pad=256)
        assert cursor[0] - at_wt >= 4 * KC * T
        at_kt = cursor[0]
        kT = sb("kT", [P, NE, T])
        qT = sb("qT", [P, NE, T])
        vb = sb("v_bias", [P, DH])
        oS = sb("o_gate", [P, NE, T])
        HO = sb("head_h", [P, NE, T])
        emt = sb("exp_minus_m", [P, SEQ])
        CO = sb("c_prompt_out", [P, NE, DH + 1])
        spl = sb("sample_small", [P, 5, NE * NS])
        st = sb("s5_sample_tmp", [P, 2, 2 * PAIRS * NS])
        wk4 = sb("wk_columns", [P, SC])
        m_out = sb("m_out", [H, 1 + NS])
        a_tile = sb("abar_tile", [P, 2, 3, 64 + PAIRS])
        at_cs = cursor[0]
        CS = sb("c_samples", [P, NS, NE, DH])
        vB = sb("v_spread", [P, NS, DH])
        assert cursor[0] <= nc.sbuf_usable_end, (cursor[0], nc.sbuf_usable_end)
        Wf = Wt[:].rearrange("p a b -> p (a b)")
        HQ = Wf[:, 0:NE * T].rearrange("p (e t) -> p e t", e=NE)
        rs = Wf[:, NE * T:(NE + 1) * T]
        vS = HO[:, 0, 0:DH]

        def smv(name):
            return sm[:, SM[name][0]:SM[name][1]]

        def curv(name):
            return cur[:, HP[name][0]:HP[name][1]]

        def hpv(name):
            return hp[:, :, HP[name][0]:HP[name][1]]

        ident = smv("ident")
        s0 = smv("s0").rearrange("p (c g b) -> p c g b", c=2, b=NS)
        n0 = smv("n0").rearrange("p (h d b) -> p h d b", h=H, d=NE)
        BR, BI = smv("b_re"), smv("b_im")
        CR, CI = smv("c_re"), smv("c_im")

        X = sb("x_tokens", [P, KC, T], at=at_cs)
        gt = [sb(f"gate_tmp{k}", [H, T], at=at_cs + 2112 * k) for k in range(10)]
        xsq = [sb(f"x_sq{k}", [P, T], at=at_wt + 2112 * k) for k in range(2)]
        xg = [sb(f"x_scaled{k}", [P, T], at=at_wt + 2112 * (2 + k)) for k in range(2)]
        rx = sb("x_rstd", [P, T], at=at_wt + 2112 * 4)
        par = sb("a_params", [P, 3, 272], at=at_kt)
        tp = [sb(f"s5_setup{k}", [P, 272], at=at_kt + 3328 + 1088 * k) for k in range(7)]
        tb = [sb(f"bbar_tmp{k}", [P, 512], at=at_ba + 2048 * k) for k in range(4)]
        sel = sb("sel_rows", [H, H, P], at=at_wt + 10560)
        r24 = sb("sample_gates", [H, 24], at=at_wt + 10560 + 2048)
        av = sb("a_row", [H, SEQ], at=at_wt + 10560 + 2048 + 128)
        HAf = sb("heads_out", [P, KC, T], at=at_wt)
        X1 = sb("x_residual", [P, KC, T], at=at_wt)
        YH = sb("s5_high", [P, 4, T], F32R, at=at_ba)
        YL = sb("s5_low", [P, 4, T], F32R, at=at_ba + 4 * 4 * T)
        sg = sb("glu_out", [P, 4, T], at=at_kt)
        HAH = sb("heads_high", [P, KC, T], F32R, at=at_small)
        at_late = cursor[0] = at_kt + 4 * 4 * T
        assert at_small + 4 * KC * T <= at_ba
        HAL = sb("heads_low", [P, KC, T], F32R)
        Y2H = sb("y2_high", [P, 4, T], F32R)
        Y2L = sb("y2_low", [P, 4, T], F32R)
        assert cursor[0] <= nc.sbuf_usable_end, ("late", cursor[0])
        MH = sb("mix_high", [P, KC, T], F32R, at=at_ba)
        t1 = sb("merge_a", [P, T], at=at_kt)
        t2 = sb("merge_b", [P, T], at=at_kt + 2112)
        t3 = sb("merge_sum", [P, T], at=at_kt + 2 * 2112)
        HIDH = sb("hidden_high", [P, F_TILES, T], F32R, at=at_small)
        HIDL = sb("hidden_low", [P, F_TILES, T], F32R, at=at_kt)
        ML = sb("mix_low", [P, KC, T], F32R, at=at_small + 4 * KC * T)
        at_tmp = at_small + 4 * F_TILES * T
        at_tmp = -(-at_tmp // 64) * 64
        ff_a = [sb(f"ff_a{k}", [P, T], at=at_tmp + 2112 * k) for k in range(2)]
        ff_b = [sb(f"ff_b{k}", [P, T], at=at_tmp + 2112 * (2 + k)) for k in range(2)]
        fr = sb("ffn_rstd", [P, T], at=at_tmp + 2112 * 4)
        fsq = [sb(f"ffn_sq{k}", [P, T], at=at_tmp + 2112 * (5 + k)) for k in range(2)]
        xs = [sb("x1_scaled", [P, T], at=at_tmp + 2112 * 7)]
        facc = sb("ffn_sq_sum", [P, T], at=at_tmp + 2112 * 8)
        xacc = sb("x_sq_sum", [P, T], at=at_kt - 2112 * 3)
        assert at_tmp + 2112 * 9 <= at_wt

        G = ctx.enter_context(nc.psum_tensor("G", [P, 4, 512], F32))
        Q = ctx.enter_context(nc.psum_tensor("Q", [P, 4, 512], F32))
        A, B = 0, 2

        x_in = [sem(f"x_in{k}") for k in range(4)]
        gb_in, par_in, sm_in = sem("gb_in"), sem("par_in"), sem("sm_in")
        w_in = [sem(f"w_in{s}") for s in range(RING)]
        w_hi, w_lo = sem("w_hi"), sem("w_lo")
        unit_done = sem("unit_done")
        sq_ready, sq_added, sq_summed = sem("sq_ready"), sem("sq_added"), sem("sq_summed")
        rx_root, xg_ready, hh_ready, hl_ready = sem("rx_root"), sem("xg_ready"), sem("hh_ready"), sem("hl_ready")
        consts, rows_in, fexp, fln, gates_ready = sem("consts"), sem("rows_in"), sem("fexp"), sem("fln"), sem("gates_ready")
        r24_raw, r24_ready, cols_done, cols_used = sem("r24_raw"), sem("r24_ready"), sem("cols_done"), sem("cols_used")
        s5_dt, s5_arg, s5_mag, s5_ang, s5_trig = sem("s5_dt"), sem("s5_arg"), sem("s5_mag"), sem("s5_ang"), sem("s5_trig")
        s5_den, s5_rden, s5_params = sem("s5_den"), sem("s5_rden"), sem("s5_params")
        dve_own, act_own, pool_own = sem("dve_own"), sem("act_own"), sem("pool_own")
        cur_ready = sem("cur_ready")
        u_ready, k0_ready, k1_ready, q0_ready, q1_ready = (sem(n) for n in ("u_ready", "k0_ready", "k1_ready", "q0_ready", "q1_ready"))
        built = sem("built")
        conv_done, conv_used = sem("conv_done"), sem("conv_used")
        x_done = sem("x_done")
        x_used = sem("x_used")
        scanned = sem("scanned")
        picked, mb_done, em_ready, exp_ready, w_ready = (sem(n) for n in ("picked", "mb_done", "em_ready", "exp_ready", "w_ready"))
        vb_in, v_ready = sem("vb_in"), sem("v_ready")
        scores_done, s_ready = sem("scores_done"), sem("s_ready")
        o0_ready, o1_ready = sem("o0_ready"), sem("o1_ready")
        num_done, den_abs, h_ready, qn_ready = sem("num_done"), sem("den_abs"), sem("h_ready"), sem("qn_ready")
        kt_done, ks_ready, c_done, co_ready = sem("kt_done"), sem("ks_ready"), sem("c_done"), sem("co_ready")
        y_done, y_raw, ys_ready = sem("y_done"), sem("y_raw"), sem("ys_ready")
        c_in, vs_out, vb_spread, c_scaled, c_new = sem("c_in"), sem("vs_out"), sem("vb_spread"), sem("c_scaled"), sem("c_new")
        smp_done, smp_used, hs_ready = sem("smp_done"), sem("smp_used"), sem("hs_ready")
        hq_ready, rms_done, rms_root, ha_ready = sem("hq_ready"), sem("rms_done"), sem("rms_root"), sem("ha_ready")
        cs_out, co_out, ha_out = sem("cs_out"), sem("co_out"), sem("ha_out")
        stores_done = sem("stores_done")
        small_out, ha_in, x1_in = sem("small_out"), sem("ha_in"), sem("x1_in")
        hah_ready, hal_ready = sem("hah_ready"), sem("hal_ready")
        yh_ready, yl_ready, glu_sig, y2h_ready, y2_raw, y2_ready = (sem(n) for n in ("yh_ready", "yl_ready", "glu_sig", "y2h_ready", "y2_raw", "y2_ready"))
        sga, wa_used, wb_used, sgb, mix_raw, mh_ready, ml_ready, curb = (sem(n) for n in ("sga", "wa_used", "wb_used", "sgb", "mix_raw", "mh_ready", "ml_ready", "curb"))
        x1_half, mrg, ffb_half = sem("x1_half"), sem("mrg"), sem("ffb_half")
        x1_ready, fsq_ready, fsq_added, fsq_summed, xs_ready, xfh_ready, xfl_ready = (sem(n) for n in ("x1_ready", "fsq_ready", "fsq_added", "fsq_summed", "xs_ready", "xfh_ready", "xfl_ready"))
        fr_root, fr_ready = sem("fr_root"), sem("fr_ready")
        ffa_ready, ffa_silu, ffb_ready, hid_raw, hidh_ready, hidl_ready = (sem(n) for n in ("ffa_ready", "ffa_silu", "ffb_ready", "hid_raw", "hidh_ready", "hidl_ready"))
        x2_ready, xsq2, x2_added, fin_root, y_ready, y_out = (sem(n) for n in ("x2_ready", "xsq2", "x2_added", "fin_root", "y_ready", "y_out"))

        block = ctx.enter_context(nc.Block())

        def bcast(ap, axis, shape):
            return ap.unsqueeze(axis).broadcast_to(shape)

        @block.sync
        def _(sp):
            for k in range(4):
                sp.dma_start(X[:, 2 * k:2 * k + 2, :], xt[:, 2 * k:2 * k + 2, :]).then_inc(x_in[k], 16)

            def load(n):
                sp.dma_start(raw[n.slot()][:], wst[bass.ds(n.val(), 1)].rearrange("a p n -> (a p) n")).then_inc(w_in[n.slot()], 16)

            for n in range(RING):
                load(At(n))
            with sp.Fori(1, N_UNITS // RING) as i:
                for s in range(RING):
                    sp.wait_ge(w_lo, RING * i + s - RING + 1)
                    load(At(s, RING, i))

        @block.scalar
        def _(act):
            own = Order(act, act_own)

            def copy(out, in_, **kw):
                return act.activation(out, in_, ACT.Copy, **kw)

            def high(n):
                act.wait_ge(w_in[n.slot()], n.visits().val(16, 16))
                copy(WH[n.slot()][:], raw[n.slot()][:]).then_inc(w_hi, 1)

            def after(n):
                act.wait_ge(unit_done, n.val(1, 1))
                high(n.plus(RING))

            act.dma_start(par[:], apar).then_inc(par_in, 16)
            act.dma_start(sm[:], small[:, 0:NSM]).then_inc(sm_in, 16)
            act.dma_start(gb[:], small[:, NSM:NSM + 44]).then_inc(gb_in, 16)
            act.wait_ge(par_in, 16)
            act.activation(par[:, 2, :], par[:, 2, :], ACT.Exp).then_inc(s5_dt, 1)
            for k in range(KC):
                act.wait_ge(x_in[k // 2], 16)
                if k >= 2:
                    act.wait_ge(sq_added, k - 1)
                act.activation(xsq[k % 2][:], X[:, k, :], ACT.Square).then_inc(sq_ready, 1)
            act.wait_ge(s5_arg, 1)
            act.activation(tp[0][:], tp[0][:], ACT.Exp).then_inc(s5_mag, 1)
            for n in range(RING):
                high(At(n))
            act.wait_ge(sq_summed, 1)
            act.wait_ge(consts, 1)
            act.activation(rx[:, 0:256], G[:, B, 0:256], ACT.Sqrt, bias=eps[:, 0:1], scale=1.0 / D).then_inc(rx_root, 1)
            act.activation(rx[:, 256:T], G[:, B + 1, 0:264], ACT.Sqrt, bias=eps[:, 0:1], scale=1.0 / D).then_inc(rx_root, 1)
            for k in range(KC):
                act.wait_ge(xg_ready, k + 1)
                copy(HH[:, k, :], xg[k % 2][:]).then_inc(hh_ready, 1)
            after(At(0))
            act.wait_ge(rows_in, 1)
            act.activation(gt[3][:], gt[2][:], ACT.Exp, scale=-1.0).then_inc(fexp, 1)
            act.wait_ge(fexp, 1)
            act.activation(gt[4][:], gt[3][:], ACT.Ln, bias=1.0).then_inc(fln, 1)
            act.wait_ge(s5_ang, 1)
            act.activation(tp[4][:], tp[1][:], ACT.Sin).then_inc(s5_trig, 1)
            act.activation(tp[5][:], tp[3][:], ACT.Sin, bias=half_pi[:, 0:1], scale=-1.0).then_inc(s5_trig, 1)
            act.wait_ge(r24_raw, 1)
            act.activation(r24[:], r24[:], ACT.Exp).then_inc(r24_ready, 1)

            with act.Fori(0, H) as i:
                n = At(N_MIX, PER_HEAD, i)
                for j in range(5):
                    after(n.plus(j))
                act.wait_ge(conv_done, i + 1)
                act.wait_ge(cur_ready, i + 1)
                for jj in range(PAIRS):
                    r = slice(32 * jj, 32 * jj + 32)
                    last = copy(Kb[r, :, r], Q[r, 0, 0:256].rearrange("p (d c) -> p d c", d=L))
                last.then_inc(conv_used, 1)
                act.wait_ge(x_done, i + 2)
                for c in range(2):
                    last = copy(S[:, c, :, 1:NCOL], Q[:, :, 72 * c:72 * c + 72])
                last.then_inc(x_used, 1)
                act.wait_ge(mb_done, i + 1)
                act.activation(emt[:], Q[:, 2, :], ACT.Exp, scale=-1.0).then_inc(em_ready, 1)
                for j in range(SC):
                    last = act.activation(Wt[:, j, P * j:SEQ], Q[:, 3, P * j:SEQ], ACT.Exp,
                                          bias=curv("acol")[:, j:j + 1], scale=-1.0)
                last.then_inc(exp_ready, 1)
                after(n.plus(5))
                after(n.plus(6))
                for e, ready in ((0, o0_ready), (1, o1_ready)):
                    act.wait_ge(unit_done, n.val(1, 8 + e))
                    pair = B if e == 0 else A
                    act.activation(oS[:, e, 0:256], G[:, pair, 0:256], ACT.Sigmoid, bias=curv("bias")[:, 5 + e:6 + e])
                    act.activation(oS[:, e, 256:T], G[:, pair + 1, 0:264], ACT.Sigmoid,
                                   bias=curv("bias")[:, 5 + e:6 + e]).then_inc(ready, 1)
                    high(n.plus(7 + e + RING))
                act.wait_ge(num_done, i + 1)
                act.activation(Wf[:, 0:SEQ], Q[:, 0, :], ACT.Abs).then_inc(den_abs, 1)
                act.wait_ge(c_in, 16 * i + 16)
                for b in range(NS):
                    last = copy(CS[:, b, :, :], CS[:, b, :, :], scale=curv("samp")[:, b:b + 1])
                last.then_inc(c_scaled, 1)
                act.wait_ge(kt_done, i + 1)
                act.wait_ge(s_ready, i + 1)
                for j in range(SC):
                    last = copy(KS[:, j, :], G[:, B + j // 2, 256 * (j % 2):256 * (j % 2) + 256], scale=wk4[:, j:j + 1])
                last.then_inc(ks_ready, 1)
                act.wait_ge(c_done, i + 1)
                act.wait_ge(stores_done, i + 1)
                for d in range(NE):
                    last = copy(CO[:, d, :], G[:, A + d, 0:DH + 1])
                last.then_inc(co_ready, 1)
                act.wait_ge(y_raw, i + 1)
                act.activation(YS[:, bass.ds(i, 1), :], uT[:].unsqueeze(1), ACT.Gelu_apprx_tanh).then_inc(ys_ready, 1)
                act.wait_ge(hs_ready, i + 1)
                act.activation(HQ, HO[:], ACT.Square).then_inc(hq_ready, 1)
                act.wait_ge(rms_done, i + 1)
                act.activation(rs[:, 0:SEQ], Q[:, 0, :], ACT.Sqrt, bias=eps[:, 0:1], scale=1.0 / DH)
                act.activation(rs[:, SEQ:T], G[:, B + 1, 0:NS], ACT.Sqrt, bias=eps[:, 0:1], scale=1.0 / DH).then_inc(rms_root, 1)

            for m in range(4):
                act.wait_ge(ys_ready, H)
                act.wait_ge(y_done, H + 1)
                act.wait_ge(smp_done, H)
                copy(YH[:, m, :], YS[:, m, :]).then_inc(yh_ready, 1)
            n = At(N_GLU)
            for m in range(4):
                if m % 2 == 1:
                    after(n.plus(m // 2))
                else:
                    act.wait_ge(glu_sig, m // 2 + 1)
                pair = A if m % 2 == 0 else B
                act.wait_ge(ha_ready, H)
                act.activation(sg[:, m, 0:256], G[:, pair, 0:256], ACT.Sigmoid, bias=b_glu[:, m:m + 1])
                act.activation(sg[:, m, 256:T], G[:, pair + 1, 0:264], ACT.Sigmoid, bias=b_glu[:, m:m + 1]).then_inc(y2_raw, 1)
            act.wait_ge(ha_in, 16)
            for k in range(KC):
                copy(HAH[:, k, :], HAf[:, k, :]).then_inc(hah_ready, 1)
            for m in range(4):
                act.wait_ge(y2_ready, m + 1)
                copy(Y2H[:, m, 0:SEQ].rearrange("p (b t) -> p b t", t=L),
                     sg[:, m, 0:SEQ].rearrange("p (t b) -> p b t", t=L))
                copy(Y2H[:, m, SEQ:T], sg[:, m, SEQ:T]).then_inc(y2h_ready, 1)

            copy(junk_a[:], eps[:]).then_inc(sgb, 1)
            for m, n in steps(act, KC, PER_MERGE, 3, N_MERGE):
                act.wait_ge(curb, m.val(1, 1))
                for g, (t, ready) in enumerate(((t1, sga), (t2, sgb))):
                    act.wait_ge(unit_done, n.val(1, 2 * g + 1))
                    act.wait_ge(ml_ready, m.val(1, 1))
                    act.activation(t[:, 0:256], G[:, A, 0:256], ACT.Sigmoid, bias=cur_b[:, g:g + 1])
                    act.activation(t[:, 256:T], G[:, A + 1, 0:264], ACT.Sigmoid, bias=cur_b[:, g:g + 1]).then_inc(ready, 1)
                    high(n.plus(2 * g + RING))
                    after(n.plus(2 * g + 1))
                act.wait_ge(mix_raw, m.val(1, 1))
                copy(MH[:, bass.ds(m.val(), 1), :], t3[:].unsqueeze(1)).then_inc(mh_ready, 1)

            for m, n in steps(act, KC, 1, 3, N_OUT):
                after(n)
                act.wait_ge(x1_ready, m.val(1, 4))
                act.wait_ge(fsq_added, m.val(1, 1))
                act.activation(fsq[0][:], X1[:, bass.ds(m.val(), 1), :].squeeze(1), ACT.Square).then_inc(fsq_ready, 1)
                act.wait_ge(xs_ready, m.val(1, 1))
                copy(HH[:, bass.ds(m.val(), 1), :], xs[0][:].unsqueeze(1)).then_inc(xfh_ready, 1)
            act.wait_ge(fsq_summed, 1)
            act.activation(fr[:, 0:256], Q[:, 2, 0:256], ACT.Sqrt, bias=eps[:, 0:1], scale=1.0 / D)
            act.activation(fr[:, 256:T], Q[:, 3, 0:264], ACT.Sqrt, bias=eps[:, 0:1], scale=1.0 / D).then_inc(fr_root, 1)
            for f, n in steps(act, F_TILES, 2, 3, N_FF):
                after(n)
                act.wait_ge(ffa_ready, f.val(1, 2))
                act.activation(ff_a[0][:], ff_a[0][:], ACT.Silu).then_inc(ffa_silu, 1)
                after(n.plus(1))
                act.wait_ge(hid_raw, f.val(1, 1))
                copy(HIDH[:, bass.ds(f.val(), 1), :], ff_b[0][:].unsqueeze(1)).then_inc(hidh_ready, 1)
            for m, n in steps(act, KC, 3, 2, N_DOWN, loops=3):
                for j in range(3):
                    if m.i is not None or m.static < KC - 1:
                        after(n.plus(j))
                act.wait_ge(x2_ready, m.val(1, 3))
                act.wait_ge(x2_added, m.val(1, 1))
                act.activation(fsq[0][:], X1[:, bass.ds(m.val(), 1), :].squeeze(1), ACT.Square).then_inc(xsq2, 1)
            act.wait_ge(fsq_summed, 2)
            act.activation(fr[:, 0:256], Q[:, 2, 0:256], ACT.Sqrt, bias=eps[:, 0:1], scale=1.0 / D)
            act.activation(fr[:, 256:T], Q[:, 3, 0:264], ACT.Sqrt, bias=eps[:, 0:1], scale=1.0 / D).then_inc(fin_root, 1)
            for m in range(KC):
                act.wait_ge(y_ready, m + 1)
                act.dma_start(y_o[:, m, :], X1[:, m, :]).then_inc(y_out, 16)
            act.wait_ge(y_out, 16 * KC)

        @block.gpsimd
        def _(pool):
            own = Order(pool, pool_own)
            tt = pool.tensor_tensor

            def mul(o, a, b):
                own.do(tt(o, a, b, ALU.mult))

            def add(o, a, b):
                own.do(tt(o, a, b, ALU.add))

            def sub(o, a, b):
                own.do(tt(o, a, b, ALU.subtract))

            def tsc(o, a, s1, op1, s2=None, op2=ALU.bypass):
                own.do(pool.tensor_scalar(o, a, s1, s2, op1, op2) if s2 is not None else pool.tensor_scalar(o, a, s1, None, op1))

            ar, ai, dt = par[:, 0, :], par[:, 1, :], par[:, 2, :]
            t = [x[:] for x in tp]
            pool.wait_ge(s5_dt, 1)
            tt(t[0], dt, ar, ALU.mult).then_inc(s5_arg, 1)
            mul(t[1], dt, ai)
            C1, C2 = 6.28125, 4058.0 / 2 ** 21
            C3 = 6.283185307179586476925 - C1 - C2
            ROUND = 1.5 * 2 ** 23
            tsc(t[2], t[1], 0.15915494309189535, ALU.mult)
            tsc(t[2], t[2], ROUND, ALU.add)
            tsc(t[2], t[2], -ROUND, ALU.add)
            for c in (C1, C2, C3):
                tsc(t[3], t[2], -c, ALU.mult)
                add(t[1], t[1], t[3])
            tsc(t[1], t[1], 3.1415925, ALU.min, -3.1415925, ALU.max)
            tsc(t[3], t[1], 0.0, ALU.max)
            tsc(t[6], t[1], 0.0, ALU.min)
            tt(t[3], t[3], t[6], ALU.subtract).then_inc(s5_ang, 1)
            mul(t[2], ar, ar)
            mul(t[6], ai, ai)
            tt(t[2], t[2], t[6], ALU.add).then_inc(s5_den, 1)
            pool.wait_ge(s5_mag, 1)
            pool.wait_ge(s5_trig, 2)
            re1, im1 = a_pow[:, 0, 0, :], a_pow[:, 1, 0, :]
            mul(re1, t[0], t[5])
            mul(im1, t[0], t[4])

            def square(ore, oim, re, im, w):
                mul(t[3][:, 0:w], re, re)
                mul(t[4][:, 0:w], im, im)
                mul(t[5][:, 0:w], re, im)
                sub(ore, t[3][:, 0:w], t[4][:, 0:w])
                tsc(oim, t[5][:, 0:w], 2.0, ALU.mult)

            for k in range(2):
                square(a_pow[:, 0, k + 1, :], a_pow[:, 1, k + 1, :], a_pow[:, 0, k, :], a_pow[:, 1, k, :], 272)
            pool.wait_ge(s5_rden, 1)
            tsc(t[3], re1, -1.0, ALU.add)
            mul(t[4], t[3], ar)
            mul(t[5], im1, ai)
            add(t[4], t[4], t[5])
            mul(t[4], t[4], t[2])
            mul(t[5], im1, ar)
            mul(t[6], t[3], ai)
            sub(t[5], t[5], t[6])
            mul(t[5], t[5], t[2])
            pool.wait_ge(sm_in, 16)
            for half in range(2):
                br, bi = BR[:, 512 * half:512 * half + 512], BI[:, 512 * half:512 * half + 512]
                if half == 0:
                    def v3(ap):
                        return ap.rearrange("p (t g q) -> p t g q", t=4, g=2)
                    fre, fim = (bcast(x[:, 0:256].rearrange("p (t q) -> p t q", t=4), 2, [P, 4, 2, 64]) for x in (t[4], t[5]))
                else:
                    def v3(ap):
                        return ap.rearrange("p (g c) -> p g c", c=32)
                    fre, fim = (bcast(x[:, 256:272], 2, [P, 16, 32]) for x in (t[4], t[5]))
                mul(v3(tb[0][:]), v3(br), fre)
                mul(v3(tb[1][:]), v3(bi), fim)
                mul(v3(tb[2][:]), v3(bi), fre)
                mul(v3(tb[3][:]), v3(br), fim)
                sub(br, tb[0][:], tb[1][:])
                add(bi, tb[2][:], tb[3][:])
            tsc(CN[:], CI, -1.0, ALU.mult)
            own.do(pool.tensor_copy(hp[:, :, 0:10], smv("hp").rearrange("p (h c) -> p h c", h=H)))
            own.do(pool.memset(hp[:, :, HP["pick"][0]:HP["pick"][1]], 0.0))
            own.do(pool.tensor_copy(hp[32:64, :, HP["pick"][0]:HP["pick"][1]], ident[32:64, 32:36].unsqueeze(2)))

            def put(name_re, name_im, level, re, im):
                a, b = HP[name_re][0] + PAIRS * level, HP[name_im][0] + 2 * PAIRS * level
                v = lambda ap: ap.rearrange("p (t j) -> p t j", t=4)
                own.do(pool.tensor_copy(hp[:, :, a:a + PAIRS], v(re)))
                own.do(pool.tensor_scalar(hp[:, :, b:b + PAIRS], v(im), -1.0, None, ALU.mult))
                own.do(pool.tensor_copy(hp[:, :, b + PAIRS:b + 2 * PAIRS], v(im)))

            put("one_re", "one_im", 0, a_pow[:, 0, 0, 256:272], a_pow[:, 1, 0, 256:272])
            pre, pim = a_pow[:, 0, 2, 256:272], a_pow[:, 1, 2, 256:272]
            for lev in range(LEVELS):
                qre, qim = t[0][:, 16 * lev:16 * lev + 16], t[1][:, 16 * lev:16 * lev + 16]
                square(qre, qim, pre, pim, 16)
                put("scan_re", "scan_im", lev, qre, qim)
                pre, pim = qre, qim
            own.do(pool.memset(Kb[:], 0.0))
            own.do(pool.memset(junk_p[:], 0.0))
            pool.memset(S[:, :, :, 0:1], 0.0).then_inc(s5_params, 1)

            p0, p1 = pt[0][:], pt[1][:]
            with pool.Fori(0, H) as i:
                OPS = 4 + 2 + 18 + 2 + 24 + 1
                own.loop(i, OPS)

                guards = [0]

                def guard(s, value):
                    g = guards[0] = guards[0] + 1
                    pool.wait_ge(s, value)
                    return tt(junk_p[:, g:g + 1], junk_p[:, 0:1], junk_p[:, 0:1], ALU.mult)

                pool.dma_start(vb[:], vbias[bass.ds(i, 1)].rearrange("a n -> (a n)").partition_broadcast(P)).then_inc(vb_in, 16)
                pool.wait_ge(x_done, i + 1)
                src = [BR[:, 0:512].rearrange("p (t n) -> p t n", t=4), BI[:, 0:512].rearrange("p (t n) -> p t n", t=4)]
                for c in range(2):
                    own.add(pool.tensor_copy(a_tile[:, c, :, 0:64], a_pow[:, c, :, bass.ds(64 * i, 64)]))
                for c in range(2):
                    own.add(pool.tensor_copy(a_tile[:, c, :, 64:64 + PAIRS], a_pow[:, c, :, bass.ds(256 + PAIRS * i, PAIRS)]))
                for c in range(2):
                    own.do(pool.tensor_copy(BA[:, c, 0:1, :], src[c][:, bass.ds(i, 1), :]))
                for lev, w in enumerate((1, 2, 4)):
                    def g3(ap):
                        return ap.rearrange("p k (g q) -> p k g q", g=2)
                    a_re, a_im = (a_tile[:, c, lev, 0:64].unsqueeze(1).unsqueeze(1).broadcast_to([P, w, 2, 64]) for c in range(2))
                    b_re, b_im = g3(BA[:, 0, 0:w, :]), g3(BA[:, 1, 0:w, :])
                    o_re, o_im = g3(BA[:, 0, w:2 * w, :]), g3(BA[:, 1, w:2 * w, :])
                    f0 = p0[:, 0:w * P].rearrange("p (k g q) -> p k g q", k=w, g=2)
                    f1 = p1[:, 0:w * P].rearrange("p (k g q) -> p k g q", k=w, g=2)
                    mul(f0, b_re, a_re)
                    mul(f1, b_im, a_im)
                    sub(o_re, f0, f1)
                    mul(f0, b_re, a_im)
                    mul(f1, b_im, a_re)
                    add(o_im, f0, f1)
                pool.wait_ge(y_done, i + 1)
                csrc = [CR.rearrange("p (t n) -> p t n", t=4), CN[:].rearrange("p (t n) -> p t n", t=4)]
                for c in range(2):
                    own.do(pool.tensor_copy(CA[:, c, 0:1, :], csrc[c][:, bass.ds(i, 1), :]))
                for lev, a, o, w in ((0, 0, 1, 1), (1, 0, 2, 2), (2, 0, 4, 4), (2, 4, 8, 1)):
                    def c3(ap):
                        return ap.rearrange("p k (g c) -> p k g c", c=32)
                    a_re, a_im = (a_tile[:, c, lev, 64:64 + PAIRS].unsqueeze(1).unsqueeze(3).broadcast_to([P, w, PAIRS, 32]) for c in range(2))
                    b_re, b_in = c3(CA[:, 0, a:a + w, :]), c3(CA[:, 1, a:a + w, :])
                    o_re, o_in = c3(CA[:, 0, o:o + w, :]), c3(CA[:, 1, o:o + w, :])
                    f0 = p0[:, 0:w * P].rearrange("p (k g c) -> p k g c", k=w, c=32)
                    f1 = p1[:, 0:w * P].rearrange("p (k g c) -> p k g c", k=w, c=32)
                    mul(f0, b_re, a_re)
                    mul(f1, b_in, a_im)
                    add(o_re, f0, f1)
                    mul(f0, b_in, a_re)
                    mul(f1, b_re, a_im)
                    sub(o_in, f0, f1)
                bsrc = [BR[:, 512:1024].rearrange("p (t n) -> p t n", t=4), BI[:, 512:1024].rearrange("p (t n) -> p t n", t=4)]
                own.do(pool.tensor_copy(BPs[:, 0:1, :], bsrc[0][:, bass.ds(i, 1), :]))
                pool.tensor_copy(BPs[:, 1:2, :], bsrc[1][:, bass.ds(i, 1), :]).then_inc(built, 1)
                pool.wait_ge(gates_ready, 1)
                pool.dma_start(CS[:].rearrange("p a b c -> p (a b c)"), c0[bass.ds(i, 1)].rearrange("a p n -> (a p) n")).then_inc(c_in, 16)
                guard(exp_ready, i + 1)
                for j in range(SC):
                    dg = Wt[:, j, P * j:P * j + P]
                    last = pool.affine_select(out=dg, in_=dg, compare_op=ALU.is_ge, fill=0.0, base=0,
                                              pattern=[[1, P]], channel_multiplier=-1)
                last.then_inc(w_ready, 1)
                guard(v_ready, i + 1)
                pool.dma_start(v_scr, vS[P - NS:P, :]).then_inc(vs_out, 16)
                guard(vs_out, 16 * i + 16)
                pool.dma_start(vB[:].rearrange("p b e -> p (b e)"), v_scr.rearrange("b e -> (b e)").partition_broadcast(P)).then_inc(vb_spread, 16)
                guard(co_ready, i + 2)
                pool.dma_start(cp_o[bass.ds(i, 1)].rearrange("a p n -> (a p) n"), CO[:].rearrange("p a b -> p (a b)")).then_inc(co_out, 16)
                guard(c_new, i + 1)
                guard(smp_done, i + 1)
                pool.dma_start(cs_o[bass.ds(i, 1)].rearrange("a p n -> (a p) n"), CS[:].rearrange("p a b c -> p (a b c)")).then_inc(cs_out, 16)
                guard(ha_ready, i + 1)
                pool.dma_start(ha_scr[:, bass.ds(2 * i, 2), :], HO[:]).then_inc(ha_out, 16)
                guard(co_out, 16 * i + 16)
                guard(ha_out, 16 * i + 16)
                guard(cs_out, 16 * i + 16).then_inc(stores_done, 1)
            own.end(H)
            pool.dma_start(mp_o, m_out[:, 0:1]).then_inc(small_out, 16)
            pool.dma_start(ms_o, m_out[:, 1:1 + NS]).then_inc(small_out, 16)
            pool.dma_start(s5p_o, s5p[:]).then_inc(small_out, 16)
            pool.dma_start(s5s_o, s0).then_inc(small_out, 16)
            pool.dma_start(ns_o, n0).then_inc(small_out, 16)
            pool.wait_ge(small_out, 80)
            pool.wait_ge(stores_done, H + 1)
            pool.dma_start(HAf[:], ha_scr).then_inc(ha_in, 16)
            pool.wait_ge(hal_ready, KC)
            pool.dma_start(X1[:], xt).then_inc(x1_in, 16)

        @block.vector
        def _(dve):
            own = Order(dve, dve_own)
            tt, ts, stt = dve.tensor_tensor, dve.tensor_scalar, dve.scalar_tensor_tensor

            def low(n):
                dve.wait_ge(w_hi, n.val(1, 1))
                tt(WL[n.slot()][:], raw[n.slot()][:], WH[n.slot()][:].bitcast(F32), ALU.subtract).then_inc(w_lo, 1)

            def done(n):
                dve.wait_ge(unit_done, n.val(1, 1))

            credits = [0]

            def credit(s, k=1):
                credits[0] += 1
                dve.memset(junk_d[:, credits[0] - 1:credits[0]], 0.0).then_inc(s, k)

            own.add(dve.memset(ones[:], 1.0))
            dve.memset(half_pi[:], 1.5707963267948966)
            dve.memset(eps[:], EPS).then_inc(consts, 1)
            credit(x_done)
            credit(y_done)
            credit(stores_done)
            dve.wait_ge(s5_den, 1)
            dve.reciprocal(tp[2][:], tp[2][:]).then_inc(s5_rden, 1)
            dve.wait_ge(sq_ready, 1)
            own.add(dve.tensor_copy(xacc[:], xsq[0][:]))
            dve.wait_ge(dve_own, own.n)
            credit(sq_added)
            for k in range(1, KC):
                dve.wait_ge(sq_ready, k + 1)
                dve.wait_ge(sq_added, k)
                tt(xacc[:], xacc[:], xsq[k % 2][:], ALU.add).then_inc(sq_added, 1)
            for n in range(RING):
                low(At(n))
            dve.wait_ge(rx_root, 2)
            own.do(dve.reciprocal(rx[:], rx[:]))
            dve.wait_ge(gb_in, 16)

            def h_low(k):
                dve.wait_ge(hh_ready, k + 1)
                tt(HL[:, k, :], xg[k % 2][:], HH[:, k, :].bitcast(F32), ALU.subtract).then_inc(hl_ready, 1)

            for k in range(KC):
                if k >= 2:
                    dve.wait_ge(hl_ready, k - 1)
                stt(xg[k % 2][:], X[:, k, :], g_mix[:, k:k + 1], rx[:], ALU.mult, ALU.mult).then_inc(xg_ready, 1)
                dve.wait_ge(xg_ready, k + 1)
                if k >= 1:
                    h_low(k - 1)
            h_low(KC - 1)

            done(At(0))
            dve.wait_ge(sm_in, 16)
            bg = smv("b_gate")
            ig, fg, ab, lf, cum, on4, mx = gt[0], gt[1], gt[2], gt[5], gt[6], gt[7], gt[8]
            for c0_, w in HALVES:
                bank = A + (c0_ > 0)
                own.add(ts(ig[:, c0_:c0_ + w], G[0:4, bank, 0:w], bg[0:4, 0:1], None, ALU.add))
                own.add(ts(fg[:, c0_:c0_ + w], G[32:36, bank, 0:w], bg[32:36, 1:2], None, ALU.add))
            own.settle()
            stt(ab[:], fg[:], -1.0, fg[:], ALU.mult, ALU.max).then_inc(rows_in, 1)
            own.add(dve.memset(on4[:], 1.0))
            own.do(ts(lf[:], fg[:], 0.0, None, ALU.min))
            low(At(RING))
            dve.wait_ge(fln, 1)
            own.do(tt(lf[:], lf[:], gt[4][:], ALU.subtract))
            own.do(dve.tensor_tensor_scan(cum[:, 0:SEQ], on4[:, 0:SEQ], lf[:, 0:SEQ], 0.0, ALU.mult, ALU.add))
            own.do(tt(av[:], ig[:, 0:SEQ], cum[:, 0:SEQ], ALU.subtract))
            own.do(dve.tensor_tensor_scan(mx[:, 0:SEQ], av[:], av[:], 0.0, ALU.max, ALU.max))
            own.add(dve.tensor_copy(rows[32:36, 0, :], mx[:, 0:SEQ]))
            own.do(tt(cum[:, 0:SEQ], cum[:, 0:SEQ], mx[:, 0:SEQ], ALU.add))
            own.add(dve.tensor_copy(rows[32:36, 1, :], cum[:, 0:SEQ]))
            own.add(dve.tensor_copy(m_out[:, 0:1], cum[:, SEQ - 1:SEQ]))
            own.do(tt(r24[:, 0:8], lf[:, SEQ:T], smv("m0")[0:4, :], ALU.add))
            own.do(tt(m_out[:, 1:1 + NS], r24[:, 0:8], ig[:, SEQ:T], ALU.max))
            own.add(tt(r24[:, 8:16], ig[:, SEQ:T], m_out[:, 1:1 + NS], ALU.subtract))
            own.add(ts(r24[:, 16:24], m_out[:, 1:1 + NS], -1.0, None, ALU.mult))
            own.do(tt(r24[:, 0:8], r24[:, 0:8], m_out[:, 1:1 + NS], ALU.subtract))
            own.do(dve.tensor_copy(sel[:], bcast(ident[0:H, 0:H], 2, [H, H, P])))
            credit(r24_raw)
            dve.wait_ge(cols_done, 1)
            dve.wait_ge(s5_params, 1)
            own.add(dve.tensor_copy(hpv("acol").rearrange("p h j -> p j h"), G[:, B, 0:SC * H].rearrange("p (j h) -> p j h", h=H)))
            own.do(dve.tensor_copy(hpv("samp"), G[:, B + 1, 0:24 * H].rearrange("p (h n) -> p h n", n=24)))
            dve.memset(V[:, :, DH:DH + 1], 1.0).then_inc(gates_ready, 1)
            credit(co_ready)
            credit(rms_root)
            dve.wait_ge(gates_ready, 1)

            with dve.Fori(0, H) as i:
                own.loop(i, 71)
                n = At(N_MIX, PER_HEAD, i)
                dve.tensor_copy(cur[:], hp[:, bass.ds(i, 1), :].squeeze(1)).then_inc(cur_ready, 1)
                dve.wait_ge(cur_ready, i + 1)
                bias, samp = curv("bias"), curv("samp")
                ts(rows[0:4, :, :], rows[32:36, :, :], cur[32:36, HP["pick"][0]:HP["pick"][1]], None, ALU.mult).then_inc(picked, 1)
                done(n)
                ub = uT[:, 0:SEQ].rearrange("p (t b) -> p b t", t=L)
                for half in range(2):
                    own.add(ts(ub[:, 32 * half:32 * half + 32, :], G[:, A + half, 0:256].rearrange("p (b t) -> p b t", t=L),
                               bias[:, 0:1], None, ALU.add))
                ts(uT[:, SEQ:T], G[:, A + 1, 256:264], bias[:, 0:1], None, ALU.add).then_inc(u_ready, 1)
                low(n.plus(RING))
                for j, (dst, e, pair, ready) in enumerate(((kT, 0, B, k0_ready), (kT, 1, A, k1_ready),
                                                           (qT, 0, B, q0_ready), (qT, 1, A, q1_ready))):
                    done(n.plus(1 + j))
                    for half, (c, w) in enumerate(HALVES):
                        args = (bias[:, 1 + j:2 + j], DH ** -0.5, ALU.add, ALU.mult) if dst is kT else (bias[:, 1 + j:2 + j], None, ALU.add)
                        last = ts(dst[:, e, c:c + w], G[:, pair + half, 0:w], *args)
                        if half == 0:
                            own.add(last)
                    last.then_inc(ready, 1)
                    if j < 3 or True:
                        low(n.plus(1 + j + RING))
                dve.wait_ge(q1_ready, i + 1)
                dve.wait_ge(k1_ready, i + 1)
                kw, t8, qn, de, rc = (spl[:, x, :].rearrange("p (d b) -> p d b", d=NE) for x in range(5))
                own.add(tt(kw, kT[:, :, SEQ:T], bcast(samp[:, 8:16], 1, [P, NE, NS]), ALU.mult))
                n_i = n0[:, bass.ds(i, 1), :, :].squeeze(1)
                own.do(tt(t8, n_i, bcast(samp[:, 0:8], 1, [P, NE, NS]), ALU.mult))
                own.do(tt(n_i, t8, kw, ALU.add))
                tt(qn, n_i, qT[:, :, SEQ:T], ALU.mult).then_inc(qn_ready, 1)

                dve.wait_ge(x_used, i + 1)

                def doubling(lev):
                    sh = 1 << lev
                    m = NB - sh
                    re = curv("scan_re")[:, PAIRS * lev:PAIRS * lev + PAIRS].unsqueeze(1).unsqueeze(3).broadcast_to([P, 2, PAIRS, m])
                    im = curv("scan_im")[:, 2 * PAIRS * lev:2 * PAIRS * (lev + 1)].rearrange("p (c j) -> p c j", c=2).unsqueeze(3).broadcast_to([P, 2, PAIRS, m])
                    src, dst = S[:, :, :, 1:1 + m], S[:, :, :, 1 + sh:1 + NB]
                    a, b = S1[:, :, :, 0:m], S2[:, :, :, 0:m]
                    own.add(tt(a, src, re, ALU.mult))
                    own.do(tt(b, S[:, ::-1, :, 1:1 + m], im, ALU.mult))
                    own.do(tt(a, a, b, ALU.add))
                    own.do(tt(dst, dst, a, ALU.add))

                for lev in range(4):
                    doubling(lev)
                dve.wait_ge(vb_in, 16 * i + 16)
                dve.wait_ge(stores_done, i + 1)
                done(n.plus(6))
                for half in range(2):
                    own.add(tt(V[:, 2 * half:2 * half + 2, 0:DH], G[:, B + half, :].rearrange("p (j e) -> p j e", j=2),
                               bcast(vb[:], 1, [P, 2, DH]), ALU.add))
                tt(vS, G[:, A, 0:DH], vb[:], ALU.add).then_inc(v_ready, 1)
                low(n.plus(5 + RING))
                low(n.plus(6 + RING))
                dve.wait_ge(w_ready, i + 1)
                dve.wait_ge(scores_done, i + 1)
                own.do(dve.tensor_copy(wk4[:], Wt[:, :, SEQ - 1]))
                for j in range(SC):
                    w = SEQ - P * j
                    q_bank, q_off = (j, 0) if j < 2 else (2, 256 * (j - 2))
                    last = tt(Wt[:, j, P * j:SEQ], Q[:, q_bank, q_off:q_off + w], Wt[:, j, P * j:SEQ], ALU.mult)
                    if j < SC - 1:
                        own.add(last)
                last.then_inc(s_ready, 1)
                doubling(4)
                doubling(5)
                g4 = bass.ds(PAIRS * i, PAIRS)
                s_i = s0[:, :, g4, :]
                u1, u2 = (st[:, x, :].rearrange("p (c j b) -> p c j b", c=2, b=NS) for x in range(2))
                own.add(tt(u1, s_i, curv("one_re").unsqueeze(1).unsqueeze(3).broadcast_to([P, 2, PAIRS, NS]), ALU.mult))
                im2 = curv("one_im").rearrange("p (c j) -> p c j", c=2)
                for c in range(2):
                    own.add(tt(u2[:, c], s0[:, 1 - c, g4, :], bcast(im2[:, c], 2, [P, PAIRS, NS]), ALU.mult))
                own.settle()
                own.do(tt(u1, u1, u2, ALU.add))
                own.do(tt(S[:, :, :, 1 + NB:NCOL], S[:, :, :, 1 + NB:NCOL], u1, ALU.add))
                own.add(dve.tensor_copy(s5p[:, :, g4], S[:, :, :, NB]))
                dve.tensor_copy(s_i, S[:, :, :, 1 + NB:NCOL]).then_inc(scanned, 1)
                done(n.plus(7))
                low(n.plus(7 + RING))
                done(n.plus(8))
                low(n.plus(8 + RING))
                dve.wait_ge(em_ready, i + 1)
                dve.wait_ge(den_abs, i + 1)
                own.do(tt(emt[:], emt[:], Wf[:, 0:SEQ], ALU.max))
                own.do(dve.reciprocal(emt[:], emt[:]))
                dve.wait_ge(vs_out, 16 * i + 16)
                own.add(tt(HO[:, 0, 0:SEQ], Q[:, 1, :], emt[:], ALU.mult))
                tt(HO[:, 1, 0:SEQ], Q[:, 2, :], emt[:], ALU.mult).then_inc(h_ready, 1)
                dve.wait_ge(vb_spread, 16 * i + 16)
                dve.wait_ge(c_scaled, i + 1)
                for b in range(NS):
                    for d in range(NE):
                        last = stt(CS[:, b, d, :], vB[:, b, :], kw[:, d, b:b + 1], CS[:, b, d, :], ALU.mult, ALU.add)
                        if b < NS - 1 or d < NE - 1:
                            own.add(last)
                last.then_inc(c_new, 1)
                dve.wait_ge(y_done, i + 2)
                dve.wait_ge(smp_done, i + 1)
                own.add(stt(uT[:, 0:SEQ], uT[:, 0:SEQ], curv("skip"), Q[:, 3, :], ALU.mult, ALU.add))
                stt(uT[:, SEQ:T], uT[:, SEQ:T], curv("skip"), G[:, B, 24:32], ALU.mult, ALU.add).then_inc(y_raw, 1)
                own.do(dve.tensor_copy(de[:, 0, :], G[:, B, 0:8]))
                own.do(stt(rc[:, 0, :], de[:, 0, :], -1.0, de[:, 0, :], ALU.mult, ALU.max))
                own.do(tt(rc[:, 0, :], rc[:, 0, :], samp[:, 16:24], ALU.max))
                own.do(dve.reciprocal(rc[:, 0, :], rc[:, 0, :]))
                tt(HO[:, :, SEQ:T], G[:, B, 8:24].rearrange("p (e b) -> p e b", e=NE), bcast(rc[:, 0, :], 1, [P, NE, NS]),
                   ALU.mult).then_inc(hs_ready, 1)
                dve.wait_ge(rms_root, i + 2)
                own.do(dve.reciprocal(rs, rs))
                for e in range(NE):
                    own.add(stt(HO[:, e, :], HO[:, e, :], curv("norm_g")[:, e:e + 1], rs, ALU.mult, ALU.mult))
                own.settle()
                dve.wait_ge(o1_ready, i + 1)
                tt(HO[:], HO[:], oS[:], ALU.mult).then_inc(ha_ready, 1)
            own.end(H)

            for m in range(4):
                dve.wait_ge(yh_ready, m + 1)
                tt(YL[:, m, :], YS[:, m, :], YH[:, m, :].bitcast(F32), ALU.subtract).then_inc(yl_ready, 1)
            n = At(N_GLU)
            for m in range(4):
                if m % 2 == 1:
                    done(n.plus(m // 2))
                    low(n.plus(m // 2 + RING))
                dve.wait_ge(y2_raw, m + 1)
                tt(sg[:, m, :], sg[:, m, :], YS[:, m, :], ALU.mult).then_inc(y2_ready, 1)
            dve.wait_ge(ha_in, 16)
            for k in range(KC):
                dve.wait_ge(hah_ready, k + 1)
                tt(HAL[:, k, :], HAf[:, k, :], HAH[:, k, :].bitcast(F32), ALU.subtract).then_inc(hal_ready, 1)
            for m in range(4):
                dve.wait_ge(y2h_ready, m + 1)
                own.add(tt(Y2L[:, m, 0:SEQ].rearrange("p (b t) -> p b t", t=L),
                           sg[:, m, 0:SEQ].rearrange("p (t b) -> p b t", t=L),
                           Y2H[:, m, 0:SEQ].rearrange("p (b t) -> p b t", t=L).bitcast(F32), ALU.subtract))
                tt(Y2L[:, m, SEQ:T], sg[:, m, SEQ:T], Y2H[:, m, SEQ:T].bitcast(F32), ALU.subtract).then_inc(yl_ready, 1)
            credit(wb_used)
            credit(ml_ready)

            for m, n in steps(dve, KC, PER_MERGE, 3, N_MERGE):
                dve.tensor_copy(cur_b[:], b_merge[:, bass.ds(m.val(2), 2)]).then_inc(curb, 1)
                done(n)
                low(n.plus(RING))
                done(n.plus(1))
                for g, (t, sig, used) in enumerate(((t1, sga, wa_used), (t2, sgb, wb_used))):
                    if g == 1:
                        done(n.plus(2))
                        low(n.plus(2 + RING))
                        done(n.plus(3))
                    dve.wait_ge(sig, m.val(1, 1 + g))
                    own_wait = used
                    tt(t[:, 0:256], t[:, 0:256], G[:, B, 0:256], ALU.mult).then_inc(mrg, 1)
                    tt(t[:, 256:T], t[:, 256:T], G[:, B + 1, 0:264], ALU.mult).then_inc(used, 1)
                    low(n.plus(2 * g + 1 + RING))
                dve.wait_ge(mrg, m.val(2, 2))
                dve.wait_ge(wa_used, m.val(1, 1))
                dve.wait_ge(wb_used, m.val(1, 2))
                dve.wait_ge(ml_ready, m.val(1, 1))
                tt(t3[:], t1[:], t2[:], ALU.add).then_inc(mix_raw, 1)
                dve.wait_ge(mh_ready, m.val(1, 1))
                mm = bass.ds(m.val(), 1)
                tt(ML[:, mm, :], t3[:].unsqueeze(1), MH[:, mm, :].bitcast(F32), ALU.subtract).then_inc(ml_ready, 1)

            dve.memset(facc[:], 0.0).then_inc(fsq_added, 1)
            credit(x1_ready, 3)
            credit(xfl_ready)
            dve.wait_ge(x1_in, 16)
            for m, n in steps(dve, KC, 1, 3, N_OUT):
                done(n)
                mm = bass.ds(m.val(), 1)
                bank = 2 * (m.static % 3)
                src = [(G if bank < 4 else Q)[:, (bank + h) % 4:(bank + h) % 4 + 1, 0:w] for h, (_, w) in enumerate(HALVES)]
                tt(X1[:, mm, 0:256], X1[:, mm, 0:256], src[0], ALU.add).then_inc(x1_half, 1)
                tt(X1[:, mm, 256:T], X1[:, mm, 256:T], src[1], ALU.add).then_inc(x1_ready, 1)
                dve.wait_ge(xfl_ready, m.val(1, 1))
                dve.tensor_copy(cur_b[:, 0:1], g_ffn[:, mm]).then_inc(curb, 1)
                dve.wait_ge(x1_half, m.val(1, 1))
                dve.wait_ge(x1_ready, m.val(1, 4))
                dve.wait_ge(curb, m.val(1, KC + 1))
                ts(xs[0][:], X1[:, mm, :].squeeze(1), cur_b[:, 0:1], None, ALU.mult).then_inc(xs_ready, 1)
                low(n.plus(RING))
                dve.wait_ge(fsq_ready, m.val(1, 1))
                dve.wait_ge(fsq_added, m.val(1, 1))
                tt(facc[:], facc[:], fsq[0][:], ALU.add).then_inc(fsq_added, 1)
                dve.wait_ge(xfh_ready, m.val(1, 1))
                tt(HL[:, mm, :], xs[0][:].unsqueeze(1), HH[:, mm, :].bitcast(F32), ALU.subtract).then_inc(xfl_ready, 1)
            credit(ffa_ready)
            credit(ffb_ready)
            credit(hidl_ready)
            dve.wait_ge(fr_root, 1)
            dve.reciprocal(fr[:], fr[:]).then_inc(fr_ready, 1)
            dve.wait_ge(fr_ready, 1)
            for f, n in steps(dve, F_TILES, 2, 3, N_FF):
                done(n)
                dve.wait_ge(hidl_ready, f.val(1, 1))
                tt(ff_a[0][:, 0:256], G[:, A, 0:256], fr[:, 0:256], ALU.mult)
                tt(ff_a[0][:, 256:T], G[:, A + 1, 0:264], fr[:, 256:T], ALU.mult).then_inc(ffa_ready, 1)
                low(n.plus(RING))
                done(n.plus(1))
                tt(ff_b[0][:, 0:256], G[:, B, 0:256], fr[:, 0:256], ALU.mult).then_inc(ffb_half, 1)
                tt(ff_b[0][:, 256:T], G[:, B + 1, 0:264], fr[:, 256:T], ALU.mult).then_inc(ffb_ready, 1)
                low(n.plus(1 + RING))
                dve.wait_ge(ffa_silu, f.val(1, 1))
                dve.wait_ge(ffb_half, f.val(1, 1))
                dve.wait_ge(ffb_ready, f.val(1, 2))
                tt(ff_b[0][:], ff_b[0][:], ff_a[0][:], ALU.mult).then_inc(hid_raw, 1)
                dve.wait_ge(hidh_ready, f.val(1, 1))
                ff = bass.ds(f.val(), 1)
                tt(HIDL[:, ff, :], ff_b[0][:].unsqueeze(1), HIDH[:, ff, :].bitcast(F32), ALU.subtract).then_inc(hidl_ready, 1)
            dve.memset(facc[:], 0.0).then_inc(x2_added, 1)
            credit(x2_ready, 2)
            for m, n in steps(dve, KC, 3, 2, N_DOWN, loops=3):
                for j in range(3):
                    if m.i is not None or m.static < KC - 1:
                        done(n.plus(j))
                        low(n.plus(j + RING))
                done(n.plus(2))
                mm = bass.ds(m.val(), 1)
                pair = A if m.static % 2 == 0 else B
                tt(X1[:, mm, 0:256], X1[:, mm, 0:256], G[:, pair:pair + 1, 0:256], ALU.add).then_inc(x1_half, 1)
                tt(X1[:, mm, 256:T], X1[:, mm, 256:T], G[:, pair + 1:pair + 2, 0:264], ALU.add).then_inc(x2_ready, 1)
                dve.wait_ge(xsq2, m.val(1, 1))
                dve.wait_ge(x2_added, m.val(1, 1))
                tt(facc[:], facc[:], fsq[0][:], ALU.add).then_inc(x2_added, 1)
            dve.wait_ge(fin_root, 1)
            dve.reciprocal(fr[:], fr[:]).then_inc(fr_ready, 1)
            dve.wait_ge(fr_ready, 2)
            for m in range(KC):
                stt(X1[:, m, :], X1[:, m, :], g_fin[:, m:m + 1], fr[:], ALU.mult, ALU.mult).then_inc(y_ready, 1)

        @block.tensor
        def _(pe):
            mm = pe.matmul

            def tiles(pair):
                t = G if pair < 4 else Q
                return [t[:, pair % 4, 0:256], t[:, pair % 4 + 1, 0:264]]

            def product(slot, hi, lo, out, cols, start=True, stop=True, ready=None, w0=0):
                n = len(cols)
                for x, k in enumerate(cols):
                    if ready is not None:
                        pe.wait_ge(ready, k + 1)
                    c = slice(P * (w0 + x), P * (w0 + x) + P)
                    for t, (w, h) in enumerate(((WH, hi), (WH, lo), (WL, hi))):
                        for o, (c0_, width) in zip(out, HALVES):
                            last = mm(o, w[slot][:, c], h[:, k, c0_:c0_ + width],
                                      start=start and x == 0 and t == 0, stop=stop and x == n - 1 and t == 2)
                return last

            def unit(n, hi, lo, pair, cols=range(KC), **kw):
                pe.wait_ge(w_lo, n.val(1, 1))
                last = product(n.slot(), hi, lo, tiles(pair), cols, **kw)
                last.then_inc(unit_done, 1)

            pe.wait_ge(sq_added, KC)
            mm(G[:, B, 0:256], ones[:], xacc[:, 0:256], start=True, stop=True)
            mm(G[:, B + 1, 0:264], ones[:], xacc[:, 256:T], start=True, stop=True).then_inc(sq_summed, 1)
            unit(At(0), HH, HL, A, ready=hl_ready)
            pe.wait_ge(r24_raw, 1)
            for j in range(SC):
                pe.transpose(G[:, B, H * j:H * j + H], av[:, P * j:P * j + P], ident[0:H, 0:H])
            pe.wait_ge(r24_ready, 1)
            for h in range(H):
                last = mm(G[:, B + 1, 24 * h:24 * h + 24], sel[:, h, :], r24[:], start=True, stop=True)
            last.then_inc(cols_done, 1)

            with pe.Fori(0, H) as i:
                n = At(N_MIX, PER_HEAD, i)
                pe.wait_ge(co_ready, i + 1)
                unit(n, HH, HL, A)
                pe.wait_ge(rms_root, i + 1)
                unit(n.plus(1), HH, HL, B)
                pe.wait_ge(u_ready, i + 1)
                unit(n.plus(2), HH, HL, A)
                pe.wait_ge(k0_ready, i + 1)
                unit(n.plus(3), HH, HL, B)
                pe.wait_ge(k1_ready, i + 1)
                unit(n.plus(4), HH, HL, A)

                pe.wait_ge(built, i + 1)
                for jj in range(PAIRS):
                    for c in range(2):
                        last = mm(Q[32 * jj:32 * jj + 32, 0, 0:256], BPs[:, c, 32 * jj:32 * jj + 32],
                                  CA[:, c, 0:L, 32 * jj:32 * jj + 32], start=c == 0, stop=c == 1)
                last.then_inc(conv_done, 1)
                pe.wait_ge(conv_used, i + 1)
                for c in range(2):
                    for x, t in enumerate(reversed(range(L))):
                        w = NB + NS if t == L - 1 else NB
                        for jj in range(PAIRS):
                            r = slice(32 * jj, 32 * jj + 32)
                            last = mm(Q[:, jj, 72 * c:72 * c + w], BA[r, c, L - 1 - t, :], uT[r, NB * t:NB * t + w],
                                      start=x == 0, stop=x == L - 1)
                last.then_inc(x_done, 1)

                pe.wait_ge(w_lo, n.val(1, 7))
                pe.wait_ge(q1_ready, i + 1)
                for tile in range(5):
                    cols = slice(P * tile, P * tile + P) if tile < 4 else slice(T - P, T)
                    out = G[:, B + tile // 2, 256 * (tile % 2):256 * (tile % 2) + 256] if tile < 4 else G[:, A, 0:256]
                    for k in range(KC):
                        sl = n.plus(5 + k // 4).slot()
                        wc = slice(256 * (k % 4), 256 * (k % 4) + 256)
                        for t, (w, h) in enumerate(((WH, HH), (WH, HL), (WL, HH))):
                            last = mm(out, h[:, k, cols], w[sl][:, wc], start=k == 0 and t == 0, stop=k == KC - 1 and t == 2)
                last.then_inc(unit_done, 2)

                pe.wait_ge(x_used, i + 1)
                pe.wait_ge(picked, i + 1)
                mm(Q[:, 3, :], ones[0:H, :], rows[0:H, 0, :], start=True, stop=True)
                mm(Q[:, 2, :], ones[0:H, :], rows[0:H, 1, :], start=True, stop=True).then_inc(mb_done, 1)
                pe.wait_ge(v_ready, i + 1)
                unit(n.plus(7), HH, HL, B)
                pe.wait_ge(em_ready, i + 1)
                for j in range(SC):
                    q_bank, q_off = (j, 0) if j < 2 else (2, 256 * (j - 2))
                    for e in range(NE):
                        last = mm(Q[:, q_bank, q_off:q_off + SEQ - P * j], kT[:, e, P * j:P * j + P], qT[:, e, P * j:SEQ],
                                  start=e == 0, stop=e == NE - 1)
                last.then_inc(scores_done, 1)
                unit(n.plus(8), HH, HL, A)
                pe.wait_ge(s_ready, i + 1)
                for j in range(SC):
                    mm(Q[:, 0, P * j:SEQ], ones[:], Wt[:, j, P * j:SEQ], start=j == 0, stop=j == SC - 1)
                for e in range(NE):
                    for j in range(SC):
                        last = mm(Q[:, 1 + e, P * j:SEQ], V[:, j, P * e:P * e + P], Wt[:, j, P * j:SEQ],
                                  start=j == 0, stop=j == SC - 1)
                last.then_inc(num_done, 1)
                pe.wait_ge(o0_ready, i + 1)
                for j in range(SC):
                    for e in range(NE):
                        last = pe.transpose(G[:, B + j // 2, 256 * (j % 2) + P * e:256 * (j % 2) + P * e + P],
                                            kT[:, e, P * j:P * j + P], ident)
                last.then_inc(kt_done, 1)
                pe.wait_ge(scanned, i + 1)
                for d in range(L):
                    mm(Q[:, 3, NB * d:SEQ], Kb[:, d, :], uT[:, 0:NB * (L - d)], start=d == 0, stop=False, skip_group_check=True)
                for t in range(L):
                    for c in range(2):
                        for jj in range(PAIRS):
                            last = mm(Q[32 * jj:32 * jj + 32, 3, NB * t:NB * t + NB], CA[:, c, t + 1, 32 * jj:32 * jj + 32],
                                      S[:, c, jj, 0:NB], start=False, stop=t == L - 1 and c == 1, skip_group_check=True)
                pe.wait_ge(ks_ready, i + 1)
                pe.wait_ge(o1_ready, i + 1)
                for d in range(NE):
                    for j in range(SC):
                        last = mm(G[:, A + d, 0:DH + 1], KS[:, j, P * d:P * d + P], V[:, j, :], start=j == 0, stop=j == SC - 1)
                last.then_inc(c_done, 1)
                for jj in range(PAIRS):
                    for c in range(2):
                        last = mm(G[32 * jj:32 * jj + 32, B, 24:32], CA[:, c, 0, 32 * jj:32 * jj + 32], S[:, c, jj, 1 + NB:NCOL],
                                  start=c == 0, stop=c == 1)
                last.then_inc(y_done, 1)
                pe.wait_ge(qn_ready, i + 1)
                for e in range(NE):
                    mm(G[:, B, 0:NS], ones[:], spl[:, 2, NS * e:NS * e + NS], start=e == 0, stop=e == NE - 1)
                pe.wait_ge(c_new, i + 1)
                for e in range(NE):
                    for b in range(NS):
                        for d in range(NE):
                            last = mm(G[:, B, 8 + NS * e + b:9 + NS * e + b], CS[:, b, d, P * e:P * e + P],
                                      qT[:, d, SEQ + b:SEQ + b + 1], start=d == 0, stop=d == NE - 1)
                last.then_inc(smp_done, 1)
                pe.wait_ge(hq_ready, i + 1)
                for e in range(NE):
                    mm(Q[:, 0, :], ones[:], HQ[:, e, 0:SEQ], start=e == 0, stop=e == NE - 1)
                for e in range(NE):
                    last = mm(G[:, B + 1, 0:NS], ones[:], HQ[:, e, SEQ:T], start=e == 0, stop=e == NE - 1)
                last.then_inc(rms_done, 1)

            for m in range(4):
                n = At(N_GLU + m // 2)
                pe.wait_ge(w_lo, n.val(1, 1))
                pe.wait_ge(yl_ready, 4)
                if m == 0:
                    pe.wait_ge(co_ready, H + 1)
                elif m == 1:
                    pe.wait_ge(rms_root, H + 1)
                else:
                    pe.wait_ge(y2_raw, m - 1)
                product(n.slot(), YH, YL, tiles(A if m % 2 == 0 else B), range(4), w0=4 * (m % 2)).then_inc(
                    glu_sig if m % 2 == 0 else unit_done, 1)
            for m, n in steps(pe, KC, PER_MERGE, 3, N_MERGE):
                pe.wait_ge(sgb, m.val(1, 1))
                unit(n, HH, HL, A)
                pe.wait_ge(wb_used, m.val(1, 1))
                pe.wait_ge(hal_ready, KC)
                unit(n.plus(1), HAH, HAL, B)
                pe.wait_ge(sga, m.val(1, 1))
                unit(n.plus(2), HH, HL, A)
                pe.wait_ge(wa_used, m.val(1, 1))
                pe.wait_ge(yl_ready, 8)
                unit(n.plus(3), Y2H, Y2L, B, cols=range(4))
            pe.wait_ge(ml_ready, KC + 1)
            for m, n in steps(pe, KC, 1, 3, N_OUT):
                pe.wait_ge(x1_ready, m.val(1, 1))
                unit(n, MH, ML, 2 * (m.static % 3))
            pe.wait_ge(fsq_added, KC + 1)
            mm(Q[:, 2, 0:256], ones[:], facc[:, 0:256], start=True, stop=True)
            mm(Q[:, 3, 0:264], ones[:], facc[:, 256:T], start=True, stop=True).then_inc(fsq_summed, 1)
            pe.wait_ge(xfl_ready, KC + 1)
            for f, n in steps(pe, F_TILES, 2, 3, N_FF):
                pe.wait_ge(ffa_ready, f.val(1, 1))
                unit(n, HH, HL, A)
                pe.wait_ge(ffb_ready, f.val(1, 1))
                unit(n.plus(1), HH, HL, B)
            pe.wait_ge(hidl_ready, F_TILES + 1)
            for m, n in steps(pe, KC, 3, 2, N_DOWN, loops=3):
                pe.wait_ge(x2_ready, m.val(1, 1))
                for j in range(3):
                    unit(n.plus(j), HIDH, HIDL, A if m.static % 2 == 0 else B, cols=range(DOWN_CUT[j], DOWN_CUT[j + 1]),
                         start=j == 0, stop=j == 2)
            pe.wait_ge(x2_added, KC + 1)
            mm(Q[:, 2, 0:256], ones[:], facc[:, 0:256], start=True, stop=True)
            mm(Q[:, 3, 0:264], ones[:], facc[:, 256:T], start=True, stop=True).then_inc(fsq_summed, 1)


def kernel(**inputs):
    import numpy as np
    import concourse.bacc as bacc
    from concourse.bass_utils import run_bass_kernel_spmd

    a = {k: np.asarray(v) for k, v in inputs.items()}
    f32 = np.float32

    def chunks(w, cols):
        return w[:, cols].reshape(-1, P, len(cols)).transpose(1, 0, 2)

    w_in, b_in = a["w_in"][0], a["b_in"][0]
    w_a, w_glu, w_b, w_out = a["w_a"][0], a["w_glu"][0], a["w_b"][0], a["w_out"][0]
    w1, w3, w2 = a["w_ff1"][0], a["w_ff3"][0], a["w_ff2"][0]
    OFF_G, OFF_U = 4 * D, 4 * D + 2 * H
    OFF_GA = OFF_U + 512
    OFF_GB = OFF_GA + D
    wst = np.zeros((N_UNITS, P, U), f32)
    tile = lambda off, m: np.arange(off + P * m, off + P * m + P)
    gates = wst[N_GATES].reshape(P, KC, P)
    gates[:, :, 0:H] = chunks(w_in, np.arange(OFF_G, OFF_G + H))
    gates[:, :, 32:32 + H] = chunks(w_in, np.arange(OFF_G + H, OFF_G + 2 * H))
    for h in range(H):
        n = N_MIX + PER_HEAD * h
        wst[n] = chunks(w_in, tile(OFF_U, h)).reshape(P, U)
        for e in range(NE):
            wst[n + 1 + e] = chunks(w_in, tile(D, NE * h + e)).reshape(P, U)
            wst[n + 3 + e] = chunks(w_in, tile(0, NE * h + e)).reshape(P, U)
            wst[n + 7 + e] = chunks(w_in, tile(3 * D, NE * h + e)).reshape(P, U)
        v = chunks(w_in, np.arange(2 * D + DH * h, 2 * D + DH * h + DH))
        wst[n + 5] = v[:, 0:4].reshape(P, U)
        wst[n + 6] = v[:, 4:8].reshape(P, U)
    for m in range(4):
        wst[N_GLU + m // 2][:, 512 * (m % 2):512 * (m % 2) + 512] = chunks(w_glu, tile(0, m)).reshape(P, 512)
    for m in range(KC):
        n = N_MERGE + PER_MERGE * m
        wst[n] = chunks(w_in, tile(OFF_GA, m)).reshape(P, U)
        wst[n + 1] = chunks(w_a, tile(0, m)).reshape(P, U)
        wst[n + 2] = chunks(w_in, tile(OFF_GB, m)).reshape(P, U)
        wst[n + 3][:, 0:512] = chunks(w_b, tile(0, m)).reshape(P, 512)
        wst[N_OUT + m] = chunks(w_out, tile(0, m)).reshape(P, U)
        down = chunks(w2, tile(0, m))
        for j in range(3):
            part = down[:, DOWN_CUT[j]:DOWN_CUT[j + 1]]
            wst[N_DOWN + 3 * m + j][:, 0:P * part.shape[1]] = part.reshape(P, -1)
    for f in range(F_TILES):
        wst[N_FF + 2 * f] = chunks(w1, tile(0, f)).reshape(P, U)
        wst[N_FF + 2 * f + 1] = chunks(w3, tile(0, f)).reshape(P, U)

    x = np.concatenate([a["x_prompt"].reshape(SEQ, D), a["x_sample"].reshape(NS, D)], axis=0)
    xt = np.ascontiguousarray(x.T.reshape(KC, P, T).transpose(1, 0, 2))

    col = lambda v: v.reshape(-1, P).T
    def s5_rows(g):
        c = np.broadcast_to(g.reshape(4, 8, 1, 64), (4, 8, 16, 64)).transpose(1, 2, 0, 3).reshape(P, 256)
        s = g.reshape(16, 2, 64).transpose(1, 2, 0).reshape(P, 16)
        return np.concatenate([c, s], axis=1)

    ldt = np.broadcast_to(a["s5_log_dt"][0][:, None], (32, 64))
    apar = np.ascontiguousarray(np.stack([s5_rows(a["s5_A_re"][0]), s5_rows(a["s5_A_im"][0]), s5_rows(ldt)], axis=1))

    def state_major(b):
        o = np.zeros((2, 64, 16, 2, 16), f32)
        v = b.reshape(16, 2, 64, 16)
        for g in range(2):
            o[g, :, :, g, :] = v[:, g].transpose(1, 0, 2)
        return o.reshape(P, 512)

    def channel_major(b):
        o = np.zeros((8, 16, 4, 2, 64), f32)
        v = b.reshape(4, 8, 64, 16)
        for g in range(8):
            o[g, :, :, g % 2, :] = v[:, g].transpose(2, 0, 1)
        return o.reshape(P, 512)

    small = np.zeros((P, NSM + 44), f32)

    def put(name, v, rows=slice(0, P)):
        small[rows, SM[name][0]:SM[name][1]] = v

    for part in ("re", "im"):
        bmat = a["s5_B_" + part][0]
        put("b_" + part, np.concatenate([channel_major(bmat), state_major(bmat)], axis=1))
        put("c_" + part, state_major(a["s5_C_" + part][0].transpose(0, 2, 1)))
    s0 = np.stack([a["state_s5_re"][0], a["state_s5_im"][0]])
    put("s0", s0.reshape(2, NS, 16, 2, 64).transpose(3, 4, 0, 2, 1).reshape(P, 256))
    put("n0", a["state_mlstm_n"][0].reshape(NS, H, NE, P).transpose(3, 1, 2, 0).reshape(P, 64))
    put("ident", np.eye(P, dtype=f32))
    put("m0", a["state_mlstm_m"][0].T, slice(0, H))
    small[0:H, SM["b_gate"][0]] = b_in[OFF_G:OFF_G + H]
    small[32:32 + H, SM["b_gate"][0] + 1] = b_in[OFF_G + H:OFF_G + 2 * H]
    hpar = np.zeros((P, H, 10), f32)
    bu, bq, bk, bo = col(b_in[OFF_U:OFF_GA]), col(b_in[0:D]), col(b_in[D:2 * D]), col(b_in[3 * D:4 * D])
    hpar[:, :, 0] = bu
    for e in range(NE):
        hpar[:, :, 1 + e], hpar[:, :, 3 + e], hpar[:, :, 5 + e] = bk[:, e::2], bq[:, e::2], bo[:, e::2]
        hpar[:, :, 8 + e] = col(a["mlstm_norm_g"][0])[:, e::2]
    hpar[:, :, 7] = col(a["s5_D"][0])
    put("hp", hpar.reshape(P, 40))
    small[:, NSM:NSM + 8] = col(a["norm_mix_g"][0])
    small[:, NSM + 8:NSM + 16] = col(a["norm_ffn_g"][0])
    small[:, NSM + 16:NSM + 24] = col(a["norm_final_g"])
    small[:, NSM + 24:NSM + 40:2] = col(b_in[OFF_GA:OFF_GB])
    small[:, NSM + 25:NSM + 40:2] = col(b_in[OFF_GB:])
    small[:, NSM + 40:NSM + 44] = col(a["b_glu"][0])
    vbias = np.ascontiguousarray(b_in[2 * D:3 * D].reshape(H, DH))
    c0 = np.ascontiguousarray(a["state_mlstm_C"][0].reshape(NS, H, NE, P, DH).transpose(1, 3, 0, 2, 4).reshape(H, P, NS * NE * DH))

    arrays = {"wst": wst, "xt": xt, "small": small, "apar": apar, "vbias": vbias, "c0": c0}
    outs = {"y": (P, KC, T), "cp": (H, P, NE * (DH + 1)), "mp": (H, 1), "s5p": (P, 2, 16),
            "cs": (H, P, NS * NE * DH), "ns": (P, H, NE, NS), "ms": (H, NS), "s5s": (P, 2, 16, NS)}
    nc = bacc.Bacc("TRN2", target_bir_lowering=False, num_devices=1)
    args = [nc.dram_tensor(k, v.shape, F32, kind="ExternalInput").ap() for k, v in arrays.items()]
    args += [nc.dram_tensor("out_" + k, s, F32, kind="ExternalOutput").ap() for k, s in outs.items()]
    build(nc, *args)
    res = run_bass_kernel_spmd(nc, [arrays], core_ids=[0]).results[0]
    r = {k: res["out_" + k] for k in outs}
    y = r["y"].transpose(1, 0, 2).reshape(D, T).T
    cp = r["cp"].reshape(H, P, NE, DH + 1).transpose(0, 2, 1, 3).reshape(H, DH, DH + 1)
    sp = r["s5p"].reshape(2, 64, 2, 16).transpose(2, 3, 0, 1).reshape(2, 1, 1, 32, 64)
    ss = r["s5s"].reshape(2, 64, 2, 16, NS).transpose(2, 4, 3, 0, 1).reshape(2, 1, NS, 32, 64)
    cs = r["cs"].reshape(H, P, NS, NE, DH).transpose(2, 0, 3, 1, 4).reshape(1, NS, H, DH, DH)
    ns = r["ns"].transpose(3, 1, 2, 0).reshape(1, NS, H, DH)
    c = np.ascontiguousarray
    return (c(y[:SEQ]).reshape(1, SEQ, D), c(y[SEQ:]).reshape(NS, 1, D),
            c(cp[:, :, :DH])[None, None], c(cp[:, :, DH])[None, None], c(r["mp"].reshape(1, 1, H)),
            c(sp[0]), c(sp[1]), c(cs), c(ns), c(r["ms"].T)[None], c(ss[0]), c(ss[1]))
```

```python
from contextlib import ExitStack

import concourse.bass as bass
from concourse import mybir

F32 = mybir.dt.float32
F32R = mybir.dt.float32r
ALU = mybir.AluOpType
ACT = mybir.ActivationFunctionType

P = 128
D = 1024
KC = D // P
SEQ, NS = 512, 8
T = SEQ + NS
HALVES = ((0, 256), (256, 264))
H, DH = 4, 256
NE = DH // P
SC = SEQ // P
F_TILES = 22
L = 8
NB = SEQ // L
LEVELS = 6
PAIRS = 4
NCOL = 1 + NB + NS
U = 1024
RING = 3
EPS = 1e-6

N_GATES = 0
N_MIX = 1
PER_HEAD = 9
N_GLU = N_MIX + PER_HEAD * H
N_MERGE = N_GLU + 2
PER_MERGE = 4
N_OUT = N_MERGE + PER_MERGE * KC
N_FF = N_OUT + KC
N_DOWN = N_FF + 2 * F_TILES
DOWN_CUT = (0, 8, 15, 22)
N_UNITS = N_DOWN + 3 * KC
assert N_UNITS % RING == 0

HP = {}
_at = 0
for _name, _n in (("bias", 7), ("skip", 1), ("norm_g", 2), ("acol", SC), ("samp", 24),
                  ("scan_re", LEVELS * PAIRS), ("scan_im", 2 * LEVELS * PAIRS),
                  ("one_re", PAIRS), ("one_im", 2 * PAIRS), ("pick", 1)):
    HP[_name] = (_at, _at + _n)
    _at += _n
NHP = _at
EARLY = HP["norm_g"][0]

SM = {}
_at = 0
for _name, _n in (("b_re", 1024), ("b_im", 1024), ("c_re", 512), ("c_im", 512),
                  ("s0", 256), ("n0", 64), ("ident", 128), ("m0", 8), ("b_gate", 2), ("hp", H * 10)):
    SM[_name] = (_at, _at + _n)
    _at += _n
NSM = _at


class At:

    def __init__(self, static, coef=0, i=None):
        self.static, self.coef, self.i = static, coef, i

    def plus(self, k):
        return At(self.static + k, self.coef, self.i)

    def val(self, scale=1, add=0):
        v = self.static * scale + add
        return v if self.i is None else self.coef * scale * self.i + v

    def slot(self):
        return self.static % RING

    def visits(self):
        return At(self.static // RING, self.coef // RING, self.i)


def steps(eng, count, per_step, body, first_unit, loops=None, peel=0):
    loops = (count - peel) // body if loops is None else loops
    for s in range(peel):
        yield At(s), At(first_unit + per_step * s)
    with eng.Fori(0, loops) as i:
        for s in range(peel, peel + body):
            yield At(s, body, i), At(first_unit + per_step * s, per_step * body, i)
    for s in range(peel + loops * body, count):
        yield At(s), At(first_unit + per_step * s)


class Order:

    def __init__(self, eng, sem):
        self.eng, self.sem, self.n, self.base, self.coef, self.i = eng, sem, 0, 0, 0, None

    def loop(self, i, coef):
        self.base, self.coef, self.i = self.n, coef, i

    def end(self, loops):
        assert self.n - self.base == self.coef, (self.n - self.base, self.coef)
        self.n, self.coef, self.i = self.base + self.coef * loops, 0, None

    def add(self, ins):
        ins.then_inc(self.sem, 1)
        self.n += 1

    def settle(self):
        self.eng.wait_ge(self.sem, self.n if self.i is None else self.coef * self.i + self.n)

    def do(self, ins):
        self.add(ins)
        self.settle()


def build(nc, wst, xt, small, apar, vbias, c0, y_o, cp_o, mp_o, s5p_o, cs_o, ns_o, ms_o, s5s_o):
    v_scr = nc.dram_tensor("v_scratch", (NS, DH), F32, kind="Internal").ap()
    ha_scr = nc.dram_tensor("heads_scratch", (P, KC, T), F32, kind="Internal").ap()

    ctx = ExitStack()
    with ctx:
        def sem(name):
            return ctx.enter_context(nc.semaphore(name))

        cursor = [-(-nc.sbuf_base // 64) * 64]

        def sb(name, shape, dt=F32, at=None, pad=0):
            n = 4
            for d in shape[1:]:
                n *= d
            if at is not None:
                assert at + n <= nc.sbuf_usable_end
                return nc.alloc_sbuf_tensor_at(name, shape, dt, offset=at)
            t = nc.alloc_sbuf_tensor_at(name, shape, dt, offset=cursor[0])
            cursor[0] += -(-(n + pad) // 64) * 64
            return t

        raw = [sb(f"raw{s}", [P, U]) for s in range(RING)]
        WH = [sb(f"w_high{s}", [P, U], F32R) for s in range(RING)]
        WL = [sb(f"w_low{s}", [P, U], F32R) for s in range(RING)]
        ones = sb("ones", [P, P])
        eps = sb("eps", [P, 1])
        half_pi = sb("half_pi", [P, 1])
        gb = sb("gains_biases", [P, 44])
        g_mix, g_ffn, g_fin, b_merge, b_glu = gb[:, 0:8], gb[:, 8:16], gb[:, 16:24], gb[:, 24:40], gb[:, 40:44]
        cur_b = sb("cur_b", [P, 2])
        junk_a = sb("unused_a", [P, 1])
        junk_p = sb("unused_p", [P, 16])
        junk_d = sb("unused_d", [P, 24])
        HH = sb("h_high", [P, KC, T], F32R)
        HL = sb("h_low", [P, KC, T], F32R)
        YS = sb("s5_out", [P, 4, T])

        at_small = cursor[0]
        sm = sb("small", [P, NSM])
        hp = sb("head_params", [P, H, NHP])
        cur = sb("cur_params", [P, NHP])
        a_pow = sb("abar_powers", [P, 2, 3, 272])
        CN = sb("c_im_negated", [P, 512])
        rows = sb("gate_rows", [2 * 32, 2, SEQ])
        BPs = sb("bbar_p", [P, 2, P // 4 * PAIRS])
        Kb = sb("conv_kernels", [P, L, P])
        at_ba = cursor[0]
        BA = sb("b_abar", [P, 2, L, P])
        CA = sb("c_abar", [P, 2, L + 1, P])
        assert cursor[0] - at_ba >= 2 * 4 * 4 * T
        S = sb("s5_state", [P, 2, PAIRS, NCOL])
        S1 = sb("s5_tmp1", [P, 2, PAIRS, NB])
        S2 = sb("s5_tmp2", [P, 2, PAIRS, NB])
        pt = [sb(f"pool_tmp{k}", [P, 4 * P]) for k in range(2)]
        uT = sb("uT", [P, T])
        s5p = sb("s5_prompt_out", [P, 2, 16])
        at_wt = cursor[0]
        Wt = sb("attn_weights", [P, SC, SEQ])
        KS = sb("k_scaled", [P, SC, DH])
        V = sb("V", [P, SC, DH + 1], pad=256)
        assert cursor[0] - at_wt >= 4 * KC * T
        at_kt = cursor[0]
        kT = sb("kT", [P, NE, T])
        qT = sb("qT", [P, NE, T])
        vb = sb("v_bias", [P, DH])
        at_os = cursor[0]
        oS = sb("o_gate", [P, NE, T])
        HO = sb("head_h", [P, NE, T])
        emt = sb("exp_minus_m", [P, SEQ])
        CO = sb("c_prompt_out", [P, NE, DH + 1])
        spl = sb("sample_small", [P, 5, NE * NS])
        st = sb("s5_sample_tmp", [P, 2, 2 * PAIRS * NS])
        wk4 = sb("wk_columns", [P, SC])
        m_out = sb("m_out", [H, 1 + NS])
        a_tile = sb("abar_tile", [P, 2, 3, 64 + PAIRS])
        at_cs = cursor[0]
        CS = sb("c_samples", [P, NS, NE, DH])
        at_vb = cursor[0]
        BAQ = sb("b_abar_by_step", [P, PAIRS, 2, 2, P], at=cursor[0])
        vB = sb("v_spread", [P, NS, DH])
        UQ = sb("u_by_step", [P, PAIRS, 2, NB + NS])
        assert cursor[0] <= nc.sbuf_usable_end, (cursor[0], nc.sbuf_usable_end)
        Wf = Wt[:].rearrange("p a b -> p (a b)")
        HQ = Wf[:, 0:NE * T].rearrange("p (e t) -> p e t", e=NE)
        rs = Wf[:, NE * T:(NE + 1) * T]
        vS = HO[:, 0, 0:DH]

        def smv(name):
            return sm[:, SM[name][0]:SM[name][1]]

        def curv(name):
            return cur[:, HP[name][0]:HP[name][1]]

        def hpv(name):
            return hp[:, :, HP[name][0]:HP[name][1]]

        ident = smv("ident")
        s0 = smv("s0").rearrange("p (c g b) -> p c g b", c=2, b=NS)
        n0 = smv("n0").rearrange("p (h d b) -> p h d b", h=H, d=NE)
        BR, BI = smv("b_re"), smv("b_im")
        CR, CI = smv("c_re"), smv("c_im")

        X = sb("x_tokens", [P, KC, T], at=at_cs)
        gt = [sb(f"gate_tmp{k}", [H, T], at=at_cs + 2112 * k) for k in range(10)]
        xsq = [sb(f"x_sq{k}", [P, T], at=at_wt + 2112 * k) for k in range(2)]
        xg = [sb(f"x_scaled{k}", [P, T], at=at_wt + 2112 * (2 + k)) for k in range(2)]
        rx = sb("x_rstd", [P, T], at=at_wt + 2112 * 4)
        par = sb("a_params", [P, 3, 272], at=at_os)
        tp = [sb(f"s5_setup{k}", [P, 272], at=at_os + 3328 + 1088 * k) for k in range(7)]
        tb = [sb(f"bbar_tmp{k}", [P, 512], at=at_ba + 2048 * k) for k in range(4)]
        tb2 = [sb(f"bbar_tmp_b{k}", [P, 512], at=at_vb + 2048 * k) for k in range(4)]
        sel = sb("sel_rows", [H, H, P], at=at_wt + 10560)
        r24 = sb("sample_gates", [H, 24], at=at_wt + 10560 + 2048)
        av = sb("a_row", [H, SEQ], at=at_wt + 10560 + 2048 + 128)
        HAf = sb("heads_out", [P, KC, T], at=at_wt)
        X1 = sb("x_residual", [P, KC, T], at=at_wt)
        YH = sb("s5_high", [P, 4, T], F32R, at=at_ba)
        YL = sb("s5_low", [P, 4, T], F32R, at=at_ba + 4 * 4 * T)
        sg = sb("glu_out", [P, 4, T], at=at_kt)
        HAH = sb("heads_high", [P, KC, T], F32R, at=at_small)
        Y2H = sb("y2_high", [P, 4, T], F32R, at=at_small + 4 * KC * T)
        Y2L = sb("y2_low", [P, 4, T], F32R, at=at_small + 4 * KC * T + 4 * 4 * T)
        assert at_small + 2 * 4 * KC * T <= at_ba
        at_late = cursor[0] = at_kt + 4 * 4 * T
        assert at_small + 4 * KC * T <= at_ba
        HAL = sb("heads_low", [P, KC, T], F32R)
        ML = sb("mix_low", [P, KC, T], F32R)
        assert cursor[0] <= nc.sbuf_usable_end, ("late", cursor[0])
        MH = sb("mix_high", [P, KC, T], F32R, at=at_ba)
        t1 = sb("merge_a", [P, T], at=at_kt)
        t2 = sb("merge_b", [P, T], at=at_kt + 2112)
        t3 = sb("merge_sum", [P, T], at=at_kt + 2 * 2112)
        HIDH = sb("hidden_high", [P, F_TILES, T], F32R, at=at_small)
        HIDL = sb("hidden_low", [P, F_TILES, T], F32R, at=at_kt)
        at_tmp = at_small + 4 * F_TILES * T
        at_tmp = -(-at_tmp // 64) * 64
        ff_a = [sb(f"ff_a{k}", [P, T], at=at_tmp + 2112 * k) for k in range(2)]
        ff_b = [sb(f"ff_b{k}", [P, T], at=at_tmp + 2112 * (2 + k)) for k in range(2)]
        fr = sb("ffn_rstd", [P, T], at=at_tmp + 2112 * 4)
        fsq = [sb(f"ffn_sq{k}", [P, T], at=at_tmp + 2112 * (5 + k)) for k in range(2)]
        xs = [sb("x1_scaled", [P, T], at=at_tmp + 2112 * 7)]
        facc = sb("ffn_sq_sum", [P, T], at=at_tmp + 2112 * 8)
        xacc = sb("x_sq_sum", [P, T], at=at_kt - 2112 * 3)
        assert at_tmp + 2112 * 9 <= at_wt

        G = ctx.enter_context(nc.psum_tensor("G", [P, 4, 512], F32))
        Q = ctx.enter_context(nc.psum_tensor("Q", [P, 4, 512], F32))
        A, B = 0, 2

        x_in = [sem(f"x_in{k}") for k in range(4)]
        gb_in, par_in, sm_in = sem("gb_in"), sem("par_in"), sem("sm_in")
        w_in = [sem(f"w_in{s}") for s in range(RING)]
        w_hi, w_lo = sem("w_hi"), sem("w_lo")
        unit_done = sem("unit_done")
        sq_ready, sq_added, sq_summed = sem("sq_ready"), sem("sq_added"), sem("sq_summed")
        rx_root, xg_ready, hh_ready, hl_ready = sem("rx_root"), sem("xg_ready"), sem("hh_ready"), sem("hl_ready")
        consts, rows_in, fexp, fln, gates_ready = sem("consts"), sem("rows_in"), sem("fexp"), sem("fln"), sem("gates_ready")
        r24_raw, r24_ready, cols_done, cols_used = sem("r24_raw"), sem("r24_ready"), sem("cols_done"), sem("cols_used")
        s5_dt, s5_arg, s5_mag, s5_ang, s5_trig = sem("s5_dt"), sem("s5_arg"), sem("s5_mag"), sem("s5_ang"), sem("s5_trig")
        s5_den, s5_rden, s5_params = sem("s5_den"), sem("s5_rden"), sem("s5_params")
        pow_ready, f_ready, bbar_ready = sem("pow_ready"), sem("f_ready"), sem("bbar_ready")
        dve_own, act_own, pool_own = sem("dve_own"), sem("act_own"), sem("pool_own")
        cur_ready, cur_late = sem("cur_ready"), sem("cur_late")
        u_ready, k0_ready, k1_ready, q0_ready, q1_ready = (sem(n) for n in ("u_ready", "k0_ready", "k1_ready", "q0_ready", "q1_ready"))
        built_ba, baq_act, baq_dve, uq_ready = sem("built_ba"), sem("baq_act"), sem("baq_dve"), sem("uq_ready")
        built = sem("built")
        conv_done, conv_used = sem("conv_done"), sem("conv_used")
        x_done = sem("x_done")
        x_used = sem("x_used")
        scanned = sem("scanned")
        picked, mb_done, em_ready, exp_ready, w_ready = (sem(n) for n in ("picked", "mb_done", "em_ready", "exp_ready", "w_ready"))
        vb_in, v_ready = sem("vb_in"), sem("v_ready")
        scores_done, s_ready = sem("scores_done"), sem("s_ready")
        o0_ready, o1_ready = sem("o0_ready"), sem("o1_ready")
        num_done, den_abs, h_ready, qn_ready = sem("num_done"), sem("den_abs"), sem("h_ready"), sem("qn_ready")
        kt_done, ks_ready, c_done, co_ready = sem("kt_done"), sem("ks_ready"), sem("c_done"), sem("co_ready")
        y_done, y_raw, ys_ready = sem("y_done"), sem("y_raw"), sem("ys_ready")
        c_in, vs_out, vb_spread, c_scaled, c_new = sem("c_in"), sem("vs_out"), sem("vb_spread"), sem("c_scaled"), sem("c_new")
        smp_done, smp_used, hs_ready = sem("smp_done"), sem("smp_used"), sem("hs_ready")
        hq_ready, rms_done = sem("hq_ready"), sem("rms_done")
        rms_root, ha_ready = sem("rms_root"), sem("ha_ready")
        cs_out, co_out, ha_out = sem("cs_out"), sem("co_out"), sem("ha_out")
        stores_done = sem("stores_done")
        small_out, ha_in, x1_in = sem("small_out"), sem("ha_in"), sem("x1_in")
        hah_ready, hal_ready = sem("hah_ready"), sem("hal_ready")
        yh_ready, yl_ready, glu_sig, y2h_ready, y2_raw, y2_ready = (sem(n) for n in ("yh_ready", "yl_ready", "glu_sig", "y2h_ready", "y2_raw", "y2_ready"))
        gate1_ready, pair1_used, pair2_used, gate2_ready, mix_raw, mh_ready, ml_ready, curb = (sem(n) for n in ("gate1_ready", "pair1_used", "pair2_used", "gate2_ready", "mix_raw", "mh_ready", "ml_ready", "curb"))
        x1_half, mrg, ffb_half = sem("x1_half"), sem("mrg"), sem("ffb_half")
        x1_ready, fsq_ready, fsq_added, fsq_summed, xs_ready, xfh_ready, xfl_ready = (sem(n) for n in ("x1_ready", "fsq_ready", "fsq_added", "fsq_summed", "xs_ready", "xfh_ready", "xfl_ready"))
        fr_root, fr_ready = sem("fr_root"), sem("fr_ready")
        ffa_ready, ffa_silu, ffb_ready, hid_raw, hidh_ready, hidl_ready = (sem(n) for n in ("ffa_ready", "ffa_silu", "ffb_ready", "hid_raw", "hidh_ready", "hidl_ready"))
        x2_ready, xsq2, x2_added, fin_root, y_ready, y_out = (sem(n) for n in ("x2_ready", "xsq2", "x2_added", "fin_root", "y_ready", "y_out"))

        block = ctx.enter_context(nc.Block())

        def bcast(ap, axis, shape):
            return ap.unsqueeze(axis).broadcast_to(shape)

        def spread_ba(eng, copy, quarters, ready):
            for q in quarters:
                for jj in range(PAIRS):
                    last = copy(BAQ[32 * q:32 * q + 32, jj, :, :, :], BA[32 * jj:32 * jj + 32, :, 3 - q:L:4, :])
            last.then_inc(ready, 1)

        @block.sync
        def _(sp):
            for k in range(4):
                sp.dma_start(X[:, 2 * k:2 * k + 2, :], xt[:, 2 * k:2 * k + 2, :]).then_inc(x_in[k], 16)

            def load(n):
                sp.dma_start(raw[n.slot()][:], wst[bass.ds(n.val(), 1)].rearrange("a p n -> (a p) n")).then_inc(w_in[n.slot()], 16)

            for n in range(RING):
                load(At(n))
            with sp.Fori(1, N_UNITS // RING) as i:
                for s in range(RING):
                    sp.wait_ge(w_lo, RING * i + s - RING + 1)
                    load(At(s, RING, i))

        @block.scalar
        def _(act):
            own = Order(act, act_own)

            def copy(out, in_, **kw):
                return act.activation(out, in_, ACT.Copy, **kw)

            def high(n):
                act.wait_ge(w_in[n.slot()], n.visits().val(16, 16))
                copy(WH[n.slot()][:], raw[n.slot()][:]).then_inc(w_hi, 1)

            def after(n):
                act.wait_ge(unit_done, n.val(1, 1))
                high(n.plus(RING))

            act.dma_start(par[:], apar).then_inc(par_in, 16)
            act.dma_start(gb[:], small[:, NSM:NSM + 44]).then_inc(gb_in, 16)
            act.wait_ge(par_in, 16)
            act.activation(par[:, 2, :], par[:, 2, :], ACT.Exp).then_inc(s5_dt, 1)
            act.wait_ge(s5_arg, 1)
            act.activation(tp[0][:], tp[0][:], ACT.Exp).then_inc(s5_mag, 1)
            for k in range(KC):
                act.wait_ge(x_in[k // 2], 16)
                if k >= 2:
                    act.wait_ge(sq_added, k - 1)
                act.activation(xsq[k % 2][:], X[:, k, :], ACT.Square).then_inc(sq_ready, 1)
                if k == 1:
                    act.wait_ge(consts, 1)
                    act.wait_ge(s5_ang, 1)
                    act.activation(tp[4][:], tp[1][:], ACT.Sin).then_inc(s5_trig, 1)
                    act.activation(tp[5][:], tp[3][:], ACT.Sin, bias=half_pi[:, 0:1], scale=-1.0).then_inc(s5_trig, 1)
                if k == 4:
                    act.dma_start(sm[:], small[:, 0:NSM]).then_inc(sm_in, 16)
            for n in range(RING):
                high(At(n))
            act.wait_ge(sq_summed, 1)
            act.activation(rx[:, 0:256], G[:, B, 0:256], ACT.Sqrt, bias=eps[:, 0:1], scale=1.0 / D).then_inc(rx_root, 1)
            act.activation(rx[:, 256:T], G[:, B + 1, 0:264], ACT.Sqrt, bias=eps[:, 0:1], scale=1.0 / D).then_inc(rx_root, 1)
            for k in range(KC):
                act.wait_ge(xg_ready, k + 1)
                copy(HH[:, k, :], xg[k % 2][:]).then_inc(hh_ready, 1)
            after(At(0))
            act.wait_ge(rows_in, 1)
            act.activation(gt[3][:], gt[2][:], ACT.Exp, scale=-1.0).then_inc(fexp, 1)
            act.wait_ge(fexp, 1)
            act.activation(gt[4][:], gt[3][:], ACT.Ln, bias=1.0).then_inc(fln, 1)
            act.wait_ge(r24_raw, 1)
            act.activation(r24[:], r24[:], ACT.Exp).then_inc(r24_ready, 1)
            for j in range(2):
                after(At(N_MIX + j))

            def glu(m):
                if m % 2 == 1:
                    after(At(N_GLU + m // 2))
                else:
                    act.wait_ge(glu_sig, m // 2 + 1)
                pair = A if m % 2 == 0 else B
                act.wait_ge(smp_done, H)
                act.activation(sg[:, m, 0:256], G[:, pair, 0:256], ACT.Sigmoid, bias=b_glu[:, m:m + 1])
                act.activation(sg[:, m, 256:T], G[:, pair + 1, 0:264], ACT.Sigmoid, bias=b_glu[:, m:m + 1]).then_inc(y2_raw, 1)

            def head(i, n, last_head):
                after(n.plus(2))
                after(n.plus(3))
                act.wait_ge(bbar_ready, 1)
                act.wait_ge(built_ba, i + 1)
                spread_ba(act, lambda o, x: copy(o, x), (0, 1), baq_act)
                after(n.plus(4))
                act.wait_ge(conv_done, i + 1)
                act.wait_ge(cur_ready, i + 1)
                act.wait_ge(cur_late, i + 1)
                for jj in range(PAIRS):
                    r = slice(32 * jj, 32 * jj + 32)
                    last = copy(Kb[r, :, r], Q[r, 0, 0:256].rearrange("p (d c) -> p d c", d=L))
                last.then_inc(conv_used, 1)
                act.wait_ge(x_done, i + 1)
                for c in range(2):
                    last = copy(S[:, c, :, 1:NCOL], Q[:, :, 72 * c:72 * c + 72])
                last.then_inc(x_used, 1)
                act.wait_ge(mb_done, i + 1)
                act.activation(emt[:], Q[:, 2, :], ACT.Exp, scale=-1.0).then_inc(em_ready, 1)
                act.wait_ge(ha_ready, i + 1)
                for j in range(SC):
                    last = act.activation(Wt[:, j, P * j:SEQ], Q[:, 3, P * j:SEQ], ACT.Exp,
                                          bias=curv("acol")[:, j:j + 1], scale=-1.0)
                last.then_inc(exp_ready, 1)
                after(n.plus(5))
                after(n.plus(6))
                for e, ready in ((0, o0_ready), (1, o1_ready)):
                    act.wait_ge(unit_done, n.val(1, 8 + e))
                    pair = B if e == 0 else A
                    act.activation(oS[:, e, 0:256], G[:, pair, 0:256], ACT.Sigmoid, bias=curv("bias")[:, 5 + e:6 + e])
                    act.activation(oS[:, e, 256:T], G[:, pair + 1, 0:264], ACT.Sigmoid,
                                   bias=curv("bias")[:, 5 + e:6 + e]).then_inc(ready, 1)
                    high(n.plus(7 + e + RING))
                act.wait_ge(num_done, i + 1)
                act.activation(Wf[:, 0:SEQ], Q[:, 0, :], ACT.Abs).then_inc(den_abs, 1)
                act.wait_ge(c_in, 16 * i + 16)
                for b in range(NS):
                    last = copy(CS[:, b, :, :], CS[:, b, :, :], scale=curv("samp")[:, b:b + 1])
                last.then_inc(c_scaled, 1)
                act.wait_ge(kt_done, i + 1)
                act.wait_ge(s_ready, i + 1)
                for j in range(SC):
                    last = copy(KS[:, j, :], G[:, B + j // 2, 256 * (j % 2):256 * (j % 2) + 256], scale=wk4[:, j:j + 1])
                last.then_inc(ks_ready, 1)
                act.wait_ge(c_done, i + 1)
                act.wait_ge(stores_done, i + 1)
                for d in range(NE):
                    last = copy(CO[:, d, :], G[:, A + d, 0:DH + 1])
                last.then_inc(co_ready, 1)
                act.wait_ge(y_raw, i + 1)
                act.activation(YS[:, bass.ds(i, 1), :], uT[:].unsqueeze(1), ACT.Gelu_apprx_tanh).then_inc(ys_ready, 1)
                if not last_head:
                    after(n.plus(PER_HEAD))
                else:
                    act.wait_ge(ys_ready, H)
                    act.wait_ge(y_done, H)
                    for m in range(4):
                        copy(YH[:, m, :], YS[:, m, :]).then_inc(yh_ready, 1)
                act.wait_ge(hs_ready, i + 1)
                act.activation(HQ, HO[:], ACT.Square).then_inc(hq_ready, 1)
                if not last_head:
                    after(n.plus(PER_HEAD + 1))
                else:
                    glu(0)
                    glu(1)
                act.wait_ge(rms_done, i + 1)
                act.activation(rs[:, 0:SEQ], Q[:, 0, :], ACT.Sqrt, bias=eps[:, 0:1], scale=1.0 / DH)
                act.activation(rs[:, SEQ:T], Q[:, 2, 0:NS], ACT.Sqrt, bias=eps[:, 0:1], scale=1.0 / DH).then_inc(rms_root, 1)

            with act.Fori(0, H - 1) as i:
                head(i, At(N_MIX, PER_HEAD, i), False)
            head(H - 1, At(N_MIX + PER_HEAD * (H - 1)), True)

            glu(2)
            glu(3)
            copy(junk_a[:], eps[:]).then_inc(gate2_ready, 1)
            for m in range(4):
                act.wait_ge(y2_ready, m + 1)
                copy(Y2H[:, m, 0:SEQ].rearrange("p (b t) -> p b t", t=L),
                     sg[:, m, 0:SEQ].rearrange("p (t b) -> p b t", t=L))
                copy(Y2H[:, m, SEQ:T], sg[:, m, SEQ:T]).then_inc(y2h_ready, 1)

            for m, n in steps(act, KC, PER_MERGE, 3, N_MERGE, peel=1):
                act.wait_ge(curb, m.val(1, 1))
                for g, (t, ready) in enumerate(((t1, gate1_ready), (t2, gate2_ready))):
                    act.wait_ge(unit_done, n.val(1, 2 * g + 1))
                    act.wait_ge(ml_ready, m.val(1, 1))
                    act.activation(t[:, 0:256], G[:, A, 0:256], ACT.Sigmoid, bias=cur_b[:, g:g + 1])
                    act.activation(t[:, 256:T], G[:, A + 1, 0:264], ACT.Sigmoid, bias=cur_b[:, g:g + 1]).then_inc(ready, 1)
                    high(n.plus(2 * g + RING))
                    after(n.plus(2 * g + 1))
                    if m.i is None and m.static == 0 and g == 0:
                        act.wait_ge(small_out, 80)
                        act.wait_ge(ha_in, 16)
                        for k in range(KC):
                            copy(HAH[:, k, :], HAf[:, k, :]).then_inc(hah_ready, 1)
                act.wait_ge(mix_raw, m.val(1, 1))
                copy(MH[:, bass.ds(m.val(), 1), :], t3[:].unsqueeze(1)).then_inc(mh_ready, 1)

            for m, n in steps(act, KC, 1, 3, N_OUT):
                after(n)
                act.wait_ge(x1_ready, m.val(1, 4))
                act.wait_ge(fsq_added, m.val(1, 1))
                act.activation(fsq[0][:], X1[:, bass.ds(m.val(), 1), :].squeeze(1), ACT.Square).then_inc(fsq_ready, 1)
                act.wait_ge(xs_ready, m.val(1, 1))
                copy(HH[:, bass.ds(m.val(), 1), :], xs[0][:].unsqueeze(1)).then_inc(xfh_ready, 1)
            act.wait_ge(fsq_summed, 1)
            act.activation(fr[:, 0:256], Q[:, 2, 0:256], ACT.Sqrt, bias=eps[:, 0:1], scale=1.0 / D)
            act.activation(fr[:, 256:T], Q[:, 3, 0:264], ACT.Sqrt, bias=eps[:, 0:1], scale=1.0 / D).then_inc(fr_root, 1)
            for f, n in steps(act, F_TILES, 2, 3, N_FF):
                after(n)
                act.wait_ge(ffa_ready, f.val(1, 2))
                act.activation(ff_a[0][:], ff_a[0][:], ACT.Silu).then_inc(ffa_silu, 1)
                after(n.plus(1))
                act.wait_ge(hid_raw, f.val(1, 1))
                copy(HIDH[:, bass.ds(f.val(), 1), :], ff_b[0][:].unsqueeze(1)).then_inc(hidh_ready, 1)
            for m, n in steps(act, KC, 3, 2, N_DOWN, loops=3):
                for j in range(3):
                    if m.i is not None or m.static < KC - 1:
                        after(n.plus(j))
                act.wait_ge(x2_ready, m.val(1, 3))
                act.wait_ge(x2_added, m.val(1, 1))
                act.activation(fsq[0][:], X1[:, bass.ds(m.val(), 1), :].squeeze(1), ACT.Square).then_inc(xsq2, 1)
            act.wait_ge(fsq_summed, 2)
            act.activation(fr[:, 0:256], Q[:, 2, 0:256], ACT.Sqrt, bias=eps[:, 0:1], scale=1.0 / D)
            act.activation(fr[:, 256:T], Q[:, 3, 0:264], ACT.Sqrt, bias=eps[:, 0:1], scale=1.0 / D).then_inc(fin_root, 1)
            for m in range(KC):
                act.wait_ge(y_ready, m + 1)
                act.dma_start(y_o[:, m, :], X1[:, m, :]).then_inc(y_out, 16)
            act.wait_ge(y_out, 16 * KC)

        @block.gpsimd
        def _(pool):
            own = Order(pool, pool_own)
            tt = pool.tensor_tensor

            def mul(o, a, b):
                own.do(tt(o, a, b, ALU.mult))

            def add(o, a, b):
                own.do(tt(o, a, b, ALU.add))

            def sub(o, a, b):
                own.do(tt(o, a, b, ALU.subtract))

            def tsc(o, a, s1, op1, s2=None, op2=ALU.bypass):
                own.do(pool.tensor_scalar(o, a, s1, s2, op1, op2) if s2 is not None else pool.tensor_scalar(o, a, s1, None, op1))

            pool.memset(Kb[:], 0.0)
            pool.memset(junk_p[:], 0.0)
            pool.memset(S[:, :, :, 0:1], 0.0).then_inc(s5_params, 1)
            ar, ai, dt = par[:, 0, :], par[:, 1, :], par[:, 2, :]
            t = [x[:] for x in tp]
            pool.wait_ge(s5_dt, 1)
            tt(t[0], dt, ar, ALU.mult).then_inc(s5_arg, 1)
            mul(t[2], ar, ar)
            mul(t[6], ai, ai)
            tt(t[2], t[2], t[6], ALU.add).then_inc(s5_den, 1)
            re1, im1 = a_pow[:, 0, 0, :], a_pow[:, 1, 0, :]
            pool.wait_ge(pow_ready, 1)
            pool.wait_ge(s5_rden, 1)
            tsc(t[3], re1, -1.0, ALU.add)
            mul(t[4], t[3], ar)
            mul(t[5], im1, ai)
            add(t[4], t[4], t[5])
            mul(t[5], im1, ar)
            mul(t[6], t[3], ai)
            sub(t[5], t[5], t[6])
            mul(t[6], t[4], t[2])
            mul(t[2], t[5], t[2])
            pool.wait_ge(sm_in, 16)
            tsc(CN[:], CI, -1.0, ALU.mult)
            own.settle()
            tt(junk_p[:, 0:1], junk_p[:, 1:2], junk_p[:, 1:2], ALU.mult).then_inc(f_ready, 1)
            br, bi = BR[:, 0:512], BI[:, 0:512]

            def v3(ap):
                return ap.rearrange("p (t g q) -> p t g q", t=4, g=2)
            fre, fim = (bcast(x[:, 0:256].rearrange("p (t q) -> p t q", t=4), 2, [P, 4, 2, 64]) for x in (t[6], t[2]))
            mul(v3(tb[0][:]), v3(br), fre)
            mul(v3(tb[1][:]), v3(bi), fim)
            mul(v3(tb[2][:]), v3(bi), fre)
            mul(v3(tb[3][:]), v3(br), fim)
            sub(br, tb[0][:], tb[1][:])
            add(bi, tb[2][:], tb[3][:])


            def take_powers(i):
                for c in range(2):
                    own.add(pool.tensor_copy(a_tile[:, c, :, 0:64], a_pow[:, c, :, bass.ds(64 * i, 64)]))
                for c in range(2):
                    own.add(pool.tensor_copy(a_tile[:, c, :, 64:64 + PAIRS], a_pow[:, c, :, bass.ds(256 + PAIRS * i, PAIRS)]))
                own.settle()

            def build_ba(i):
                src = [BR[:, 0:512].rearrange("p (t n) -> p t n", t=4), BI[:, 0:512].rearrange("p (t n) -> p t n", t=4)]
                for c in range(2):
                    own.do(pool.tensor_copy(BA[:, c, 0:1, :], src[c][:, bass.ds(i, 1), :]))
                for lev, w in enumerate((1, 2, 4)):
                    def g3(ap):
                        return ap.rearrange("p k (g q) -> p k g q", g=2)
                    a_re, a_im = (a_tile[:, c, lev, 0:64].unsqueeze(1).unsqueeze(1).broadcast_to([P, w, 2, 64]) for c in range(2))
                    b_re, b_im = g3(BA[:, 0, 0:w, :]), g3(BA[:, 1, 0:w, :])
                    o_re, o_im = g3(BA[:, 0, w:2 * w, :]), g3(BA[:, 1, w:2 * w, :])
                    f0 = p0[:, 0:w * P].rearrange("p (k g q) -> p k g q", k=w, g=2)
                    f1 = p1[:, 0:w * P].rearrange("p (k g q) -> p k g q", k=w, g=2)
                    mul(f0, b_re, a_re)
                    mul(f1, b_im, a_im)
                    sub(o_re, f0, f1)
                    mul(f0, b_re, a_im)
                    mul(f1, b_im, a_re)
                    if w < 4:
                        add(o_im, f0, f1)
                    else:
                        tt(o_im, f0, f1, ALU.add).then_inc(built_ba, 1)

            def build_ca(i):
                csrc = [CR.rearrange("p (t n) -> p t n", t=4), CN[:].rearrange("p (t n) -> p t n", t=4)]
                for c in range(2):
                    own.do(pool.tensor_copy(CA[:, c, 0:1, :], csrc[c][:, bass.ds(i, 1), :]))
                for lev, a, o, w in ((0, 0, 1, 1), (1, 0, 2, 2), (2, 0, 4, 4), (2, 4, 8, 1)):
                    def c3(ap):
                        return ap.rearrange("p k (g c) -> p k g c", c=32)
                    a_re, a_im = (a_tile[:, c, lev, 64:64 + PAIRS].unsqueeze(1).unsqueeze(3).broadcast_to([P, w, PAIRS, 32]) for c in range(2))
                    b_re, b_in = c3(CA[:, 0, a:a + w, :]), c3(CA[:, 1, a:a + w, :])
                    o_re, o_in = c3(CA[:, 0, o:o + w, :]), c3(CA[:, 1, o:o + w, :])
                    f0 = p0[:, 0:w * P].rearrange("p (k g c) -> p k g c", k=w, c=32)
                    f1 = p1[:, 0:w * P].rearrange("p (k g c) -> p k g c", k=w, c=32)
                    mul(f0, b_re, a_re)
                    mul(f1, b_in, a_im)
                    add(o_re, f0, f1)
                    mul(f0, b_in, a_re)
                    mul(f1, b_re, a_im)
                    sub(o_in, f0, f1)

            def build_bp(i):
                bsrc = [BR[:, 512:1024].rearrange("p (t n) -> p t n", t=4), BI[:, 512:1024].rearrange("p (t n) -> p t n", t=4)]
                own.do(pool.tensor_copy(BPs[:, 0:1, :], bsrc[0][:, bass.ds(i, 1), :]))
                pool.tensor_copy(BPs[:, 1:2, :], bsrc[1][:, bass.ds(i, 1), :]).then_inc(built, 1)

            def head(i, last_head):
                guards = [0]

                def guard(s, value):
                    g = guards[0] = guards[0] + 1
                    pool.wait_ge(s, value)
                    return tt(junk_p[:, g:g + 1], junk_p[:, 0:1], junk_p[:, 0:1], ALU.mult)

                pool.dma_start(vb[:], vbias[bass.ds(i, 1)].rearrange("a n -> (a n)").partition_broadcast(P)).then_inc(vb_in, 16)
                pool.wait_ge(gates_ready, 1)
                pool.dma_start(CS[:].rearrange("p a b c -> p (a b c)"), c0[bass.ds(i, 1)].rearrange("a p n -> (a p) n")).then_inc(c_in, 16)
                if not last_head:
                    pool.wait_ge(x_done, i + 1)
                    take_powers(i + 1)
                    build_ba(i + 1)
                guard(exp_ready, i + 1)
                for j in range(SC):
                    dg = Wt[:, j, P * j:P * j + P]
                    last = pool.affine_select(out=dg, in_=dg, compare_op=ALU.is_ge, fill=0.0, base=0,
                                              pattern=[[1, P]], channel_multiplier=-1)
                last.then_inc(w_ready, 1)
                guard(v_ready, i + 1)
                pool.dma_start(v_scr, vS[P - NS:P, :]).then_inc(vs_out, 16)
                guard(vs_out, 16 * i + 16)
                pool.dma_start(vB[:].rearrange("p b e -> p (b e)"), v_scr.rearrange("b e -> (b e)").partition_broadcast(P)).then_inc(vb_spread, 16)
                if not last_head:
                    pool.wait_ge(built_ba, i + 2)
                    pool.wait_ge(y_done, i + 1)
                    build_ca(i + 1)
                    build_bp(i + 1)
                guard(co_ready, i + 1)
                pool.dma_start(cp_o[bass.ds(i, 1)].rearrange("a p n -> (a p) n"), CO[:].rearrange("p a b -> p (a b)")).then_inc(co_out, 16)
                guard(c_new, i + 1)
                guard(smp_done, i + 1)
                pool.dma_start(cs_o[bass.ds(i, 1)].rearrange("a p n -> (a p) n"), CS[:].rearrange("p a b c -> p (a b c)")).then_inc(cs_out, 16)
                guard(ha_ready, i + 2)
                pool.dma_start(ha_scr[:, bass.ds(2 * i, 2), :], HO[:]).then_inc(ha_out, 16)
                guard(co_out, 16 * i + 16)
                guard(ha_out, 16 * i + 16)
                if last_head:
                    pool.dma_start(HAf[:], ha_scr).then_inc(ha_in, 16)
                    pool.dma_start(mp_o, m_out[:, 0:1]).then_inc(small_out, 16)
                    pool.dma_start(ms_o, m_out[:, 1:1 + NS]).then_inc(small_out, 16)
                    pool.dma_start(s5p_o, s5p[:]).then_inc(small_out, 16)
                    pool.dma_start(s5s_o, s0).then_inc(small_out, 16)
                    pool.dma_start(ns_o, n0).then_inc(small_out, 16)
                guard(cs_out, 16 * i + 16).then_inc(stores_done, 1)

            p0, p1 = pt[0][:], pt[1][:]
            take_powers(0)
            build_ba(0)
            pool.wait_ge(built_ba, 1)
            build_ca(0)
            pool.wait_ge(bbar_ready, 1)
            build_bp(0)
            with pool.Fori(0, H - 1) as i:
                own.loop(i, 4 + 2 + 17 + 2 + 24 + 1)
                head(i, False)
            own.end(H - 1)
            head(H - 1, True)
            pool.wait_ge(small_out, 80)
            pool.wait_ge(hal_ready, KC)
            pool.dma_start(X1[:], xt).then_inc(x1_in, 16)

        @block.vector
        def _(dve):
            own = Order(dve, dve_own)
            tt, ts, stt = dve.tensor_tensor, dve.tensor_scalar, dve.scalar_tensor_tensor

            def low(n):
                dve.wait_ge(w_hi, n.val(1, 1))
                tt(WL[n.slot()][:], raw[n.slot()][:], WH[n.slot()][:].bitcast(F32), ALU.subtract).then_inc(w_lo, 1)

            def done(n):
                dve.wait_ge(unit_done, n.val(1, 1))

            credits = [0]

            def credit(s, k=1):
                credits[0] += 1
                dve.memset(junk_d[:, credits[0] - 1:credits[0]], 0.0).then_inc(s, k)

            own.add(dve.memset(ones[:], 1.0))
            own.add(dve.memset(hp[:, :, HP["pick"][0]:HP["pick"][1]], 0.0))
            dve.memset(half_pi[:], 1.5707963267948966)
            dve.memset(eps[:], EPS).then_inc(consts, 1)
            credit(stores_done)
            credit(rms_root)
            credit(ha_ready)
            def tsc(o, a, s1, op1, s2=None, op2=ALU.bypass):
                own.do(ts(o, a, s1, s2, op1, op2) if s2 is not None else ts(o, a, s1, None, op1))

            ai, dt = par[:, 1, :], par[:, 2, :]
            t = [x[:] for x in tp]
            dve.wait_ge(s5_dt, 1)
            own.do(tt(t[1], dt, ai, ALU.mult))
            C1, C2 = 6.28125, 4058.0 / 2 ** 21
            C3 = 6.283185307179586476925 - C1 - C2
            ROUND = 1.5 * 2 ** 23
            tsc(t[4], t[1], 0.15915494309189535, ALU.mult)
            tsc(t[4], t[4], ROUND, ALU.add)
            tsc(t[4], t[4], -ROUND, ALU.add)
            for c in (C1, C2, C3):
                tsc(t[3], t[4], -c, ALU.mult)
                own.do(tt(t[1], t[1], t[3], ALU.add))
            tsc(t[1], t[1], 3.1415925, ALU.min, -3.1415925, ALU.max)
            tsc(t[3], t[1], 0.0, ALU.max)
            tsc(t[5], t[1], 0.0, ALU.min)
            tt(t[3], t[3], t[5], ALU.subtract).then_inc(s5_ang, 1)
            dve.wait_ge(s5_den, 1)
            dve.reciprocal(tp[2][:], tp[2][:]).then_inc(s5_rden, 1)
            dve.wait_ge(sq_ready, 1)
            own.add(dve.tensor_copy(xacc[:], xsq[0][:]))
            dve.wait_ge(dve_own, own.n)
            credit(sq_added)
            for k in range(1, KC):
                dve.wait_ge(sq_ready, k + 1)
                dve.wait_ge(sq_added, k)
                tt(xacc[:], xacc[:], xsq[k % 2][:], ALU.add).then_inc(sq_added, 1)
            dve.wait_ge(s5_mag, 1)
            dve.wait_ge(s5_trig, 2)
            re1, im1 = a_pow[:, 0, 0, :], a_pow[:, 1, 0, :]
            own.do(tt(re1, t[0], t[5], ALU.mult))
            own.do(tt(im1, t[0], t[4], ALU.mult))

            def square(ore, oim, re, im, w):
                own.do(tt(t[3][:, 0:w], re, re, ALU.mult))
                own.do(tt(t[4][:, 0:w], im, im, ALU.mult))
                own.do(tt(t[5][:, 0:w], re, im, ALU.mult))
                own.do(tt(ore, t[3][:, 0:w], t[4][:, 0:w], ALU.subtract))
                tsc(oim, t[5][:, 0:w], 2.0, ALU.mult)

            for k in range(2):
                square(a_pow[:, 0, k + 1, :], a_pow[:, 1, k + 1, :], a_pow[:, 0, k, :], a_pow[:, 1, k, :], 272)
            credit(pow_ready)
            low(At(0))
            dve.wait_ge(rx_root, 2)
            own.do(dve.reciprocal(rx[:], rx[:]))
            dve.wait_ge(gb_in, 16)

            def h_low(k):
                dve.wait_ge(hh_ready, k + 1)
                tt(HL[:, k, :], xg[k % 2][:], HH[:, k, :].bitcast(F32), ALU.subtract).then_inc(hl_ready, 1)

            for k in range(KC):
                if k >= 2:
                    dve.wait_ge(hl_ready, k - 1)
                stt(xg[k % 2][:], X[:, k, :], g_mix[:, k:k + 1], rx[:], ALU.mult, ALU.mult).then_inc(xg_ready, 1)
                dve.wait_ge(xg_ready, k + 1)
                if k >= 1:
                    h_low(k - 1)
                if k in (4, 6):
                    low(At(k // 2 - 1))
            h_low(KC - 1)

            done(At(0))
            dve.wait_ge(sm_in, 16)
            bg = smv("b_gate")
            ig, fg, ab, lf, cum, on4, mx = gt[0], gt[1], gt[2], gt[5], gt[6], gt[7], gt[8]
            for c0_, w in HALVES:
                bank = A + (c0_ > 0)
                own.add(ts(ig[:, c0_:c0_ + w], G[0:4, bank, 0:w], bg[0:4, 0:1], None, ALU.add))
                own.add(ts(fg[:, c0_:c0_ + w], G[32:36, bank, 0:w], bg[32:36, 1:2], None, ALU.add))
            own.add(dve.tensor_copy(hp[:, :, 0:10], smv("hp").rearrange("p (h c) -> p h c", h=H)))
            own.add(dve.tensor_copy(hp[32:64, :, HP["pick"][0]:HP["pick"][1]], ident[32:64, 32:36].unsqueeze(2)))
            own.settle()
            stt(ab[:], fg[:], -1.0, fg[:], ALU.mult, ALU.max).then_inc(rows_in, 1)
            own.add(dve.memset(on4[:], 1.0))
            own.do(ts(lf[:], fg[:], 0.0, None, ALU.min))
            low(At(RING))
            dve.wait_ge(fln, 1)
            own.do(tt(lf[:], lf[:], gt[4][:], ALU.subtract))
            own.do(dve.tensor_tensor_scan(cum[:, 0:SEQ], on4[:, 0:SEQ], lf[:, 0:SEQ], 0.0, ALU.mult, ALU.add))
            own.do(tt(av[:], ig[:, 0:SEQ], cum[:, 0:SEQ], ALU.subtract))
            own.do(dve.tensor_tensor_scan(mx[:, 0:SEQ], av[:], av[:], 0.0, ALU.max, ALU.max))
            own.add(dve.tensor_copy(rows[32:36, 0, :], mx[:, 0:SEQ]))
            own.do(tt(cum[:, 0:SEQ], cum[:, 0:SEQ], mx[:, 0:SEQ], ALU.add))
            own.add(dve.tensor_copy(rows[32:36, 1, :], cum[:, 0:SEQ]))
            own.add(dve.tensor_copy(m_out[:, 0:1], cum[:, SEQ - 1:SEQ]))
            own.do(tt(r24[:, 0:8], lf[:, SEQ:T], smv("m0")[0:4, :], ALU.add))
            own.do(tt(m_out[:, 1:1 + NS], r24[:, 0:8], ig[:, SEQ:T], ALU.max))
            own.add(tt(r24[:, 8:16], ig[:, SEQ:T], m_out[:, 1:1 + NS], ALU.subtract))
            own.add(ts(r24[:, 16:24], m_out[:, 1:1 + NS], -1.0, None, ALU.mult))
            own.do(tt(r24[:, 0:8], r24[:, 0:8], m_out[:, 1:1 + NS], ALU.subtract))
            own.do(dve.tensor_copy(sel[:], bcast(ident[0:H, 0:H], 2, [H, H, P])))
            credit(r24_raw)
            bias, samp = curv("bias"), curv("samp")

            def early(i, n, first=False):
                if not first:
                    dve.wait_ge(o1_ready, i)
                    dve.wait_ge(ys_ready, i)
                dve.tensor_copy(cur[:, 0:EARLY], hp[:, bass.ds(i, 1), 0:EARLY].squeeze(1)).then_inc(cur_ready, 1)
                dve.wait_ge(cur_ready, i + 1)
                done(n)
                ub = uT[:, 0:SEQ].rearrange("p (t b) -> p b t", t=L)
                for half in range(2):
                    own.add(ts(ub[:, 32 * half:32 * half + 32, :], G[:, B + half, 0:256].rearrange("p (b t) -> p b t", t=L),
                               bias[:, 0:1], None, ALU.add))
                ts(uT[:, SEQ:T], G[:, B + 1, 256:264], bias[:, 0:1], None, ALU.add).then_inc(u_ready, 1)
                low(n.plus(RING))

            def k_or_q(n, j):
                dst, e, pair, ready = ((kT, 0, A, k0_ready), (kT, 1, B, k1_ready), (qT, 0, A, q0_ready), (qT, 1, B, q1_ready))[j]
                done(n.plus(1 + j))
                for half, (c, w) in enumerate(HALVES):
                    args = (bias[:, 1 + j:2 + j], DH ** -0.5, ALU.add, ALU.mult) if dst is kT else (bias[:, 1 + j:2 + j], None, ALU.add)
                    last = ts(dst[:, e, c:c + w], G[:, pair + half, 0:w], *args)
                    if half == 0:
                        own.add(last)
                last.then_inc(ready, 1)
                low(n.plus(1 + j + RING))

            early(0, At(N_MIX), first=True)
            k_or_q(At(N_MIX), 0)

            dve.wait_ge(f_ready, 1)
            br, bi = BR[:, 512:1024], BI[:, 512:1024]

            def v3(ap):
                return ap.rearrange("p (g c) -> p g c", c=32)
            fre, fim = (bcast(x[:, 256:272], 2, [P, 16, 32]) for x in (tp[6], tp[2]))
            own.add(tt(v3(tb2[0][:]), v3(br), fre, ALU.mult))
            own.add(tt(v3(tb2[1][:]), v3(bi), fim, ALU.mult))
            own.add(tt(v3(tb2[2][:]), v3(bi), fre, ALU.mult))
            own.do(tt(v3(tb2[3][:]), v3(br), fim, ALU.mult))
            own.add(tt(br, tb2[0][:], tb2[1][:], ALU.subtract))
            own.do(tt(bi, tb2[2][:], tb2[3][:], ALU.add))
            dve.memset(UQ[:], 0.0).then_inc(bbar_ready, 1)
            def put(name_re, name_im, level, re, im):
                a, b = HP[name_re][0] + PAIRS * level, HP[name_im][0] + 2 * PAIRS * level
                v = lambda ap: ap.rearrange("p (t j) -> p t j", t=4)
                own.add(dve.tensor_copy(hp[:, :, a:a + PAIRS], v(re)))
                own.add(ts(hp[:, :, b:b + PAIRS], v(im), -1.0, None, ALU.mult))
                own.add(dve.tensor_copy(hp[:, :, b + PAIRS:b + 2 * PAIRS], v(im)))

            put("one_re", "one_im", 0, a_pow[:, 0, 0, 256:272], a_pow[:, 1, 0, 256:272])
            pre, pim = a_pow[:, 0, 2, 256:272], a_pow[:, 1, 2, 256:272]
            for lev in range(LEVELS):
                qre, qim = tp[0][:, 16 * lev:16 * lev + 16], tp[1][:, 16 * lev:16 * lev + 16]
                own.add(tt(tp[3][:, 0:16], pre, pre, ALU.mult))
                own.add(tt(tp[4][:, 0:16], pim, pim, ALU.mult))
                own.do(tt(tp[5][:, 0:16], pre, pim, ALU.mult))
                own.add(tt(qre, tp[3][:, 0:16], tp[4][:, 0:16], ALU.subtract))
                own.do(ts(qim, tp[5][:, 0:16], 2.0, None, ALU.mult))
                put("scan_re", "scan_im", lev, qre, qim)
                pre, pim = qre, qim
            dve.wait_ge(cols_done, 1)
            own.add(dve.tensor_copy(hpv("acol").rearrange("p h j -> p j h"), Q[:, 0, 0:SC * H].rearrange("p (j h) -> p j h", h=H)))
            own.do(dve.tensor_copy(hpv("samp"), Q[:, 1, 0:24 * H].rearrange("p (h n) -> p h n", n=24)))
            dve.memset(V[:, :, DH:DH + 1], 1.0).then_inc(gates_ready, 1)
            dve.wait_ge(gates_ready, 1)

            def head(i, n, last_head):
                k_or_q(n, 1)
                ut = uT[:, 0:SEQ].rearrange("p (h q b) -> p h q b", h=2, q=4)
                for jj in range(PAIRS):
                    r = slice(32 * jj, 32 * jj + 32)
                    for q in range(4):
                        own.add(dve.tensor_copy(UQ[32 * q:32 * q + 32, jj, :, 0:NB], ut[r, :, q, :]))
                    last = dve.tensor_copy(UQ[96:128, jj, 1, NB:NB + NS], uT[r, SEQ:T])
                    if jj < PAIRS - 1:
                        own.add(last)
                last.then_inc(uq_ready, 1)
                k_or_q(n, 2)
                dve.wait_ge(built_ba, i + 1)
                spread_ba(dve, dve.tensor_copy, (2, 3), baq_dve)
                k_or_q(n, 3)
                dve.wait_ge(s5_params, 1)
                dve.wait_ge(ha_ready, i + 1)
                dve.tensor_copy(cur[:, EARLY:NHP], hp[:, bass.ds(i, 1), EARLY:NHP].squeeze(1)).then_inc(cur_late, 1)
                dve.wait_ge(cur_late, i + 1)
                ts(rows[0:4, :, :], rows[32:36, :, :], cur[32:36, HP["pick"][0]:HP["pick"][1]], None, ALU.mult).then_inc(picked, 1)
                dve.wait_ge(q1_ready, i + 1)
                dve.wait_ge(k1_ready, i + 1)
                kw, t8, qn, de, rc = (spl[:, x, :].rearrange("p (d b) -> p d b", d=NE) for x in range(5))
                own.add(tt(kw, kT[:, :, SEQ:T], bcast(samp[:, 8:16], 1, [P, NE, NS]), ALU.mult))
                n_i = n0[:, bass.ds(i, 1), :, :].squeeze(1)
                own.do(tt(t8, n_i, bcast(samp[:, 0:8], 1, [P, NE, NS]), ALU.mult))
                own.do(tt(n_i, t8, kw, ALU.add))
                tt(qn, n_i, qT[:, :, SEQ:T], ALU.mult).then_inc(qn_ready, 1)

                dve.wait_ge(x_used, i + 1)

                def doubling(lev):
                    sh = 1 << lev
                    m = NB - sh
                    re = curv("scan_re")[:, PAIRS * lev:PAIRS * lev + PAIRS].unsqueeze(1).unsqueeze(3).broadcast_to([P, 2, PAIRS, m])
                    im = curv("scan_im")[:, 2 * PAIRS * lev:2 * PAIRS * (lev + 1)].rearrange("p (c j) -> p c j", c=2).unsqueeze(3).broadcast_to([P, 2, PAIRS, m])
                    src, dst = S[:, :, :, 1:1 + m], S[:, :, :, 1 + sh:1 + NB]
                    a, b = S1[:, :, :, 0:m], S2[:, :, :, 0:m]
                    own.add(tt(a, src, re, ALU.mult))
                    own.do(tt(b, S[:, ::-1, :, 1:1 + m], im, ALU.mult))
                    own.do(tt(a, a, b, ALU.add))
                    own.do(tt(dst, dst, a, ALU.add))

                for lev in range(4):
                    doubling(lev)
                dve.wait_ge(vb_in, 16 * i + 16)
                dve.wait_ge(stores_done, i + 1)
                done(n.plus(6))
                for half in range(2):
                    own.add(tt(V[:, 2 * half:2 * half + 2, 0:DH], G[:, A + half, :].rearrange("p (j e) -> p j e", j=2),
                               bcast(vb[:], 1, [P, 2, DH]), ALU.add))
                tt(vS, G[:, B, 0:DH], vb[:], ALU.add).then_inc(v_ready, 1)
                low(n.plus(5 + RING))
                low(n.plus(6 + RING))
                dve.wait_ge(w_ready, i + 1)
                dve.wait_ge(scores_done, i + 1)
                own.do(dve.tensor_copy(wk4[:], Wt[:, :, SEQ - 1]))
                for j in range(SC):
                    w = SEQ - P * j
                    q_bank, q_off = (j, 0) if j < 2 else (2, 256 * (j - 2))
                    last = tt(Wt[:, j, P * j:SEQ], Q[:, q_bank, q_off:q_off + w], Wt[:, j, P * j:SEQ], ALU.mult)
                    if j < SC - 1:
                        own.add(last)
                last.then_inc(s_ready, 1)
                doubling(4)
                doubling(5)
                g4 = bass.ds(PAIRS * i, PAIRS)
                s_i = s0[:, :, g4, :]
                u1, u2 = (st[:, x, :].rearrange("p (c j b) -> p c j b", c=2, b=NS) for x in range(2))
                own.add(tt(u1, s_i, curv("one_re").unsqueeze(1).unsqueeze(3).broadcast_to([P, 2, PAIRS, NS]), ALU.mult))
                im2 = curv("one_im").rearrange("p (c j) -> p c j", c=2)
                for c in range(2):
                    own.add(tt(u2[:, c], s0[:, 1 - c, g4, :], bcast(im2[:, c], 2, [P, PAIRS, NS]), ALU.mult))
                own.settle()
                own.do(tt(u1, u1, u2, ALU.add))
                own.do(tt(S[:, :, :, 1 + NB:NCOL], S[:, :, :, 1 + NB:NCOL], u1, ALU.add))
                own.add(dve.tensor_copy(s5p[:, :, g4], S[:, :, :, NB]))
                dve.tensor_copy(s_i, S[:, :, :, 1 + NB:NCOL]).then_inc(scanned, 1)
                done(n.plus(7))
                low(n.plus(7 + RING))
                done(n.plus(8))
                low(n.plus(8 + RING))
                dve.wait_ge(em_ready, i + 1)
                dve.wait_ge(den_abs, i + 1)
                own.do(tt(emt[:], emt[:], Wf[:, 0:SEQ], ALU.max))
                own.do(dve.reciprocal(emt[:], emt[:]))
                dve.wait_ge(vs_out, 16 * i + 16)
                own.add(tt(HO[:, 0, 0:SEQ], Q[:, 1, :], emt[:], ALU.mult))
                tt(HO[:, 1, 0:SEQ], Q[:, 2, :], emt[:], ALU.mult).then_inc(h_ready, 1)
                dve.wait_ge(vb_spread, 16 * i + 16)
                dve.wait_ge(c_scaled, i + 1)
                for b in range(NS):
                    for d in range(NE):
                        last = stt(CS[:, b, d, :], vB[:, b, :], kw[:, d, b:b + 1], CS[:, b, d, :], ALU.mult, ALU.add)
                        if b < NS - 1 or d < NE - 1:
                            own.add(last)
                last.then_inc(c_new, 1)
                dve.wait_ge(y_done, i + 1)
                own.add(stt(uT[:, 0:SEQ], uT[:, 0:SEQ], curv("skip"), Q[:, 3, :], ALU.mult, ALU.add))
                stt(uT[:, SEQ:T], uT[:, SEQ:T], curv("skip"), Q[:, 1, 24:32], ALU.mult, ALU.add).then_inc(y_raw, 1)
                if not last_head:
                    early(i + 1, n.plus(PER_HEAD))
                else:
                    for m in range(4):
                        dve.wait_ge(yh_ready, m + 1)
                        tt(YL[:, m, :], YS[:, m, :], YH[:, m, :].bitcast(F32), ALU.subtract).then_inc(yl_ready, 1)
                dve.wait_ge(smp_done, i + 1)
                own.do(dve.tensor_copy(de[:, 0, :], Q[:, 1, 0:8]))
                own.do(stt(rc[:, 0, :], de[:, 0, :], -1.0, de[:, 0, :], ALU.mult, ALU.max))
                own.do(tt(rc[:, 0, :], rc[:, 0, :], samp[:, 16:24], ALU.max))
                own.do(dve.reciprocal(rc[:, 0, :], rc[:, 0, :]))
                tt(HO[:, :, SEQ:T], Q[:, 2, 8:24].rearrange("p (e b) -> p e b", e=NE), bcast(rc[:, 0, :], 1, [P, NE, NS]),
                   ALU.mult).then_inc(hs_ready, 1)
                if not last_head:
                    k_or_q(n.plus(PER_HEAD), 0)
                else:
                    done(At(N_GLU))
                    low(At(N_GLU + RING))
                dve.wait_ge(rms_root, i + 2)
                own.do(dve.reciprocal(rs, rs))
                for e in range(NE):
                    own.add(stt(HO[:, e, :], HO[:, e, :], curv("norm_g")[:, e:e + 1], rs, ALU.mult, ALU.mult))
                own.settle()
                dve.wait_ge(o1_ready, i + 1)
                tt(HO[:], HO[:], oS[:], ALU.mult).then_inc(ha_ready, 1)

            with dve.Fori(0, H - 1) as i:
                own.loop(i, 71 + 19)
                head(i, At(N_MIX, PER_HEAD, i), False)
            own.end(H - 1)
            head(H - 1, At(N_MIX + PER_HEAD * (H - 1)), True)

            for m in range(4):
                if m == 3:
                    done(At(N_GLU + 1))
                    low(At(N_GLU + 1 + RING))
                dve.wait_ge(y2_raw, m + 1)
                tt(sg[:, m, :], sg[:, m, :], YS[:, m, :], ALU.mult).then_inc(y2_ready, 1)
            for m in range(4):
                dve.wait_ge(y2h_ready, m + 1)
                own.add(tt(Y2L[:, m, 0:SEQ].rearrange("p (b t) -> p b t", t=L),
                           sg[:, m, 0:SEQ].rearrange("p (t b) -> p b t", t=L),
                           Y2H[:, m, 0:SEQ].rearrange("p (b t) -> p b t", t=L).bitcast(F32), ALU.subtract))
                tt(Y2L[:, m, SEQ:T], sg[:, m, SEQ:T], Y2H[:, m, SEQ:T].bitcast(F32), ALU.subtract).then_inc(yl_ready, 1)
            credit(pair2_used)
            credit(ml_ready)

            for m, n in steps(dve, KC, PER_MERGE, 3, N_MERGE, peel=1):
                dve.tensor_copy(cur_b[:], b_merge[:, bass.ds(m.val(2), 2)]).then_inc(curb, 1)
                done(n)
                low(n.plus(RING))
                done(n.plus(1))
                for g, (t, sig, used) in enumerate(((t1, gate1_ready, pair1_used), (t2, gate2_ready, pair2_used))):
                    if g == 1:
                        done(n.plus(2))
                        low(n.plus(2 + RING))
                        done(n.plus(3))
                    dve.wait_ge(sig, m.val(1, 1 + g))
                    own_wait = used
                    tt(t[:, 0:256], t[:, 0:256], G[:, B, 0:256], ALU.mult).then_inc(mrg, 1)
                    tt(t[:, 256:T], t[:, 256:T], G[:, B + 1, 0:264], ALU.mult).then_inc(used, 1)
                    low(n.plus(2 * g + 1 + RING))
                    if m.i is None and m.static == 0 and g == 0:
                        dve.wait_ge(stores_done, H + 1)
                        for k in range(KC):
                            dve.wait_ge(hah_ready, k + 1)
                            tt(HAL[:, k, :], HAf[:, k, :], HAH[:, k, :].bitcast(F32), ALU.subtract).then_inc(hal_ready, 1)
                dve.wait_ge(mrg, m.val(2, 2))
                dve.wait_ge(pair1_used, m.val(1, 1))
                dve.wait_ge(pair2_used, m.val(1, 2))
                dve.wait_ge(ml_ready, m.val(1, 1))
                tt(t3[:], t1[:], t2[:], ALU.add).then_inc(mix_raw, 1)
                dve.wait_ge(mh_ready, m.val(1, 1))
                mm = bass.ds(m.val(), 1)
                tt(ML[:, mm, :], t3[:].unsqueeze(1), MH[:, mm, :].bitcast(F32), ALU.subtract).then_inc(ml_ready, 1)

            dve.memset(facc[:], 0.0).then_inc(fsq_added, 1)
            credit(x1_ready, 3)
            credit(xfl_ready)
            dve.wait_ge(x1_in, 16)
            for m, n in steps(dve, KC, 1, 3, N_OUT):
                done(n)
                mm = bass.ds(m.val(), 1)
                bank = 2 * (m.static % 3)
                src = [(G if bank < 4 else Q)[:, (bank + h) % 4:(bank + h) % 4 + 1, 0:w] for h, (_, w) in enumerate(HALVES)]
                tt(X1[:, mm, 0:256], X1[:, mm, 0:256], src[0], ALU.add).then_inc(x1_half, 1)
                tt(X1[:, mm, 256:T], X1[:, mm, 256:T], src[1], ALU.add).then_inc(x1_ready, 1)
                dve.wait_ge(xfl_ready, m.val(1, 1))
                dve.tensor_copy(cur_b[:, 0:1], g_ffn[:, mm]).then_inc(curb, 1)
                dve.wait_ge(x1_half, m.val(1, 1))
                dve.wait_ge(x1_ready, m.val(1, 4))
                dve.wait_ge(curb, m.val(1, KC + 1))
                ts(xs[0][:], X1[:, mm, :].squeeze(1), cur_b[:, 0:1], None, ALU.mult).then_inc(xs_ready, 1)
                low(n.plus(RING))
                dve.wait_ge(fsq_ready, m.val(1, 1))
                dve.wait_ge(fsq_added, m.val(1, 1))
                tt(facc[:], facc[:], fsq[0][:], ALU.add).then_inc(fsq_added, 1)
                dve.wait_ge(xfh_ready, m.val(1, 1))
                tt(HL[:, mm, :], xs[0][:].unsqueeze(1), HH[:, mm, :].bitcast(F32), ALU.subtract).then_inc(xfl_ready, 1)
            credit(ffa_ready)
            credit(ffb_ready)
            credit(hidl_ready)
            dve.wait_ge(fr_root, 1)
            dve.reciprocal(fr[:], fr[:]).then_inc(fr_ready, 1)
            dve.wait_ge(fr_ready, 1)
            for f, n in steps(dve, F_TILES, 2, 3, N_FF):
                done(n)
                dve.wait_ge(hidl_ready, f.val(1, 1))
                tt(ff_a[0][:, 0:256], G[:, A, 0:256], fr[:, 0:256], ALU.mult)
                tt(ff_a[0][:, 256:T], G[:, A + 1, 0:264], fr[:, 256:T], ALU.mult).then_inc(ffa_ready, 1)
                low(n.plus(RING))
                done(n.plus(1))
                tt(ff_b[0][:, 0:256], G[:, B, 0:256], fr[:, 0:256], ALU.mult).then_inc(ffb_half, 1)
                tt(ff_b[0][:, 256:T], G[:, B + 1, 0:264], fr[:, 256:T], ALU.mult).then_inc(ffb_ready, 1)
                low(n.plus(1 + RING))
                dve.wait_ge(ffa_silu, f.val(1, 1))
                dve.wait_ge(ffb_half, f.val(1, 1))
                dve.wait_ge(ffb_ready, f.val(1, 2))
                tt(ff_b[0][:], ff_b[0][:], ff_a[0][:], ALU.mult).then_inc(hid_raw, 1)
                dve.wait_ge(hidh_ready, f.val(1, 1))
                ff = bass.ds(f.val(), 1)
                tt(HIDL[:, ff, :], ff_b[0][:].unsqueeze(1), HIDH[:, ff, :].bitcast(F32), ALU.subtract).then_inc(hidl_ready, 1)
            dve.memset(facc[:], 0.0).then_inc(x2_added, 1)
            credit(x2_ready, 2)
            for m, n in steps(dve, KC, 3, 2, N_DOWN, loops=3):
                for j in range(3):
                    if m.i is not None or m.static < KC - 1:
                        done(n.plus(j))
                        low(n.plus(j + RING))
                done(n.plus(2))
                mm = bass.ds(m.val(), 1)
                pair = A if m.static % 2 == 0 else B
                tt(X1[:, mm, 0:256], X1[:, mm, 0:256], G[:, pair:pair + 1, 0:256], ALU.add).then_inc(x1_half, 1)
                tt(X1[:, mm, 256:T], X1[:, mm, 256:T], G[:, pair + 1:pair + 2, 0:264], ALU.add).then_inc(x2_ready, 1)
                dve.wait_ge(xsq2, m.val(1, 1))
                dve.wait_ge(x2_added, m.val(1, 1))
                tt(facc[:], facc[:], fsq[0][:], ALU.add).then_inc(x2_added, 1)
            dve.wait_ge(fin_root, 1)
            dve.reciprocal(fr[:], fr[:]).then_inc(fr_ready, 1)
            dve.wait_ge(fr_ready, 2)
            for m in range(KC):
                stt(X1[:, m, :], X1[:, m, :], g_fin[:, m:m + 1], fr[:], ALU.mult, ALU.mult).then_inc(y_ready, 1)

        @block.tensor
        def _(pe):
            mm = pe.matmul

            def tiles(pair):
                t = G if pair < 4 else Q
                return [t[:, pair % 4, 0:256], t[:, pair % 4 + 1, 0:264]]

            def product(slot, hi, lo, out, cols, start=True, stop=True, ready=None, past=0, w0=0):
                n = len(cols)
                for x, k in enumerate(cols):
                    if ready is not None:
                        pe.wait_ge(ready, k + 1 + past)
                    c = slice(P * (w0 + x), P * (w0 + x) + P)
                    for t, (w, h) in enumerate(((WH, hi), (WH, lo), (WL, hi))):
                        for o, (c0_, width) in zip(out, HALVES):
                            last = mm(o, w[slot][:, c], h[:, k, c0_:c0_ + width],
                                      start=start and x == 0 and t == 0, stop=stop and x == n - 1 and t == 2)
                return last

            def unit(n, hi, lo, pair, cols=range(KC), **kw):
                pe.wait_ge(w_lo, n.val(1, 1))
                last = product(n.slot(), hi, lo, tiles(pair), cols, **kw)
                last.then_inc(unit_done, 1)

            pe.wait_ge(sq_added, KC)
            mm(G[:, B, 0:256], ones[:], xacc[:, 0:256], start=True, stop=True)
            mm(G[:, B + 1, 0:264], ones[:], xacc[:, 256:T], start=True, stop=True).then_inc(sq_summed, 1)
            unit(At(0), HH, HL, A, ready=hl_ready)
            unit(At(N_MIX), HH, HL, B)
            pe.wait_ge(rows_in, 1)
            unit(At(N_MIX + 1), HH, HL, A)
            pe.wait_ge(r24_raw, 1)
            for j in range(SC):
                pe.transpose(Q[:, 0, H * j:H * j + H], av[:, P * j:P * j + P], ident[0:H, 0:H])
            pe.wait_ge(r24_ready, 1)
            for h in range(H):
                last = mm(Q[:, 1, 24 * h:24 * h + 24], sel[:, h, :], r24[:], start=True, stop=True)
            last.then_inc(cols_done, 1)

            def glu(m):
                n = At(N_GLU + m // 2)
                pe.wait_ge(w_lo, n.val(1, 1))
                pe.wait_ge(yl_ready, 4)
                if m == 0:
                    pe.wait_ge(co_ready, H)
                elif m == 1:
                    pe.wait_ge(ks_ready, H)
                else:
                    pe.wait_ge(y2_raw, m - 1)
                product(n.slot(), YH, YL, tiles(A if m % 2 == 0 else B), range(4), w0=4 * (m % 2)).then_inc(
                    glu_sig if m % 2 == 0 else unit_done, 1)

            def head(i, n, last_head):
                pe.wait_ge(u_ready, i + 1)
                unit(n.plus(2), HH, HL, B)
                pe.wait_ge(k0_ready, i + 1)
                unit(n.plus(3), HH, HL, A)
                pe.wait_ge(k1_ready, i + 1)
                unit(n.plus(4), HH, HL, B)

                pe.wait_ge(gates_ready, 1)
                pe.wait_ge(rms_root, i + 1)
                pe.wait_ge(built, i + 1)
                for jj in range(PAIRS):
                    for c in range(2):
                        last = mm(Q[32 * jj:32 * jj + 32, 0, 0:256], BPs[:, c, 32 * jj:32 * jj + 32],
                                  CA[:, c, 0:L, 32 * jj:32 * jj + 32], start=c == 0, stop=c == 1)
                last.then_inc(conv_done, 1)
                pe.wait_ge(w_lo, n.val(1, 7))
                pe.wait_ge(q0_ready, i + 1)

                def v_tile(tile):
                    cols = slice(P * tile, P * tile + P) if tile < 4 else slice(T - P, T)
                    out = G[:, A + tile // 2, 256 * (tile % 2):256 * (tile % 2) + 256] if tile < 4 else G[:, B, 0:256]
                    for k in range(KC):
                        sl = n.plus(5 + k // 4).slot()
                        wc = slice(256 * (k % 4), 256 * (k % 4) + 256)
                        for t, (w, h) in enumerate(((WH, HH), (WH, HL), (WL, HH))):
                            last = mm(out, h[:, k, cols], w[sl][:, wc], start=k == 0 and t == 0, stop=k == KC - 1 and t == 2)
                    return last

                v_tile(0)
                pe.wait_ge(conv_used, i + 1)
                pe.wait_ge(uq_ready, i + 1)
                pe.wait_ge(baq_act, i + 1)
                pe.wait_ge(baq_dve, i + 1)
                for jj in range(PAIRS):
                    for c in range(2):
                        mm(Q[:, jj, 72 * c:72 * c + NB + NS], BAQ[:, jj, c, 0, :], UQ[:, jj, 1, :], start=True, stop=False)
                        last = mm(Q[:, jj, 72 * c:72 * c + NB], BAQ[:, jj, c, 1, :], UQ[:, jj, 0, 0:NB], start=False, stop=True)
                last.then_inc(x_done, 1)

                for tile in range(1, 5):
                    if tile == 4:
                        pe.wait_ge(q1_ready, i + 1)
                    last = v_tile(tile)
                last.then_inc(unit_done, 2)

                pe.wait_ge(x_used, i + 1)
                pe.wait_ge(picked, i + 1)
                mm(Q[:, 3, :], ones[0:H, :], rows[0:H, 0, :], start=True, stop=True)
                mm(Q[:, 2, :], ones[0:H, :], rows[0:H, 1, :], start=True, stop=True).then_inc(mb_done, 1)
                pe.wait_ge(v_ready, i + 1)
                unit(n.plus(7), HH, HL, B)
                pe.wait_ge(em_ready, i + 1)
                for j in range(SC):
                    q_bank, q_off = (j, 0) if j < 2 else (2, 256 * (j - 2))
                    for e in range(NE):
                        last = mm(Q[:, q_bank, q_off:q_off + SEQ - P * j], kT[:, e, P * j:P * j + P], qT[:, e, P * j:SEQ],
                                  start=e == 0, stop=e == NE - 1)
                last.then_inc(scores_done, 1)
                unit(n.plus(8), HH, HL, A)
                pe.wait_ge(s_ready, i + 1)
                for j in range(SC):
                    mm(Q[:, 0, P * j:SEQ], ones[:], Wt[:, j, P * j:SEQ], start=j == 0, stop=j == SC - 1)
                for e in range(NE):
                    for j in range(SC):
                        last = mm(Q[:, 1 + e, P * j:SEQ], V[:, j, P * e:P * e + P], Wt[:, j, P * j:SEQ],
                                  start=j == 0, stop=j == SC - 1)
                last.then_inc(num_done, 1)
                pe.wait_ge(o0_ready, i + 1)
                for j in range(SC):
                    for e in range(NE):
                        last = pe.transpose(G[:, B + j // 2, 256 * (j % 2) + P * e:256 * (j % 2) + P * e + P],
                                            kT[:, e, P * j:P * j + P], ident)
                last.then_inc(kt_done, 1)
                pe.wait_ge(scanned, i + 1)
                for d in range(L):
                    mm(Q[:, 3, NB * d:SEQ], Kb[:, d, :], uT[:, 0:NB * (L - d)], start=d == 0, stop=False, skip_group_check=True)
                for t in range(L):
                    for c in range(2):
                        for jj in range(PAIRS):
                            last = mm(Q[32 * jj:32 * jj + 32, 3, NB * t:NB * t + NB], CA[:, c, t + 1, 32 * jj:32 * jj + 32],
                                      S[:, c, jj, 0:NB], start=False, stop=t == L - 1 and c == 1, skip_group_check=True)
                pe.wait_ge(ks_ready, i + 1)
                pe.wait_ge(o1_ready, i + 1)
                for d in range(NE):
                    for j in range(SC):
                        last = mm(G[:, A + d, 0:DH + 1], KS[:, j, P * d:P * d + P], V[:, j, :], start=j == 0, stop=j == SC - 1)
                last.then_inc(c_done, 1)
                pe.wait_ge(h_ready, i + 1)
                for jj in range(PAIRS):
                    for c in range(2):
                        mm(Q[32 * jj:32 * jj + 32, 1, 24:32], CA[:, c, 0, 32 * jj:32 * jj + 32], S[:, c, jj, 1 + NB:NCOL],
                           start=c == 0, stop=c == 1)
                pe.wait_ge(qn_ready, i + 1)
                for e in range(NE):
                    last = mm(Q[:, 1, 0:NS], ones[:], spl[:, 2, NS * e:NS * e + NS], start=e == 0, stop=e == NE - 1)
                last.then_inc(y_done, 1)
                if not last_head:
                    unit(n.plus(PER_HEAD), HH, HL, B)
                pe.wait_ge(c_new, i + 1)
                for e in range(NE):
                    for b in range(NS):
                        for d in range(NE):
                            last = mm(Q[:, 2, 8 + NS * e + b:9 + NS * e + b], CS[:, b, d, P * e:P * e + P],
                                      qT[:, d, SEQ + b:SEQ + b + 1], start=d == 0, stop=d == NE - 1)
                last.then_inc(smp_done, 1)
                if not last_head:
                    pe.wait_ge(co_ready, i + 1)
                    unit(n.plus(PER_HEAD + 1), HH, HL, A)
                else:
                    glu(0)
                    glu(1)
                pe.wait_ge(hq_ready, i + 1)
                for e in range(NE):
                    mm(Q[:, 0, :], ones[:], HQ[:, e, 0:SEQ], start=e == 0, stop=e == NE - 1)
                for e in range(NE):
                    last = mm(Q[:, 2, 0:NS], ones[:], HQ[:, e, SEQ:T], start=e == 0, stop=e == NE - 1)
                last.then_inc(rms_done, 1)

            with pe.Fori(0, H - 1) as i:
                head(i, At(N_MIX, PER_HEAD, i), False)
            head(H - 1, At(N_MIX + PER_HEAD * (H - 1)), True)

            glu(2)
            glu(3)
            for m, n in steps(pe, KC, PER_MERGE, 3, N_MERGE):
                pe.wait_ge(gate2_ready, m.val(1, 1))
                unit(n, HH, HL, A)
                pe.wait_ge(pair2_used, m.val(1, 1))
                pe.wait_ge(yl_ready, 8)
                unit(n.plus(1), Y2H, Y2L, B, cols=range(4))
                pe.wait_ge(gate1_ready, m.val(1, 1))
                unit(n.plus(2), HH, HL, A)
                pe.wait_ge(pair1_used, m.val(1, 1))
                pe.wait_ge(hal_ready, KC)
                unit(n.plus(3), HAH, HAL, B)
            pe.wait_ge(pair2_used, KC + 1)
            for m, n in steps(pe, KC, 1, 3, N_OUT, peel=2):
                if m.i is None and m.static == 0:
                    unit(n, MH, ML, 0, ready=ml_ready, past=1)
                else:
                    pe.wait_ge(x1_ready, m.val(1, 1))
                    unit(n, MH, ML, 2 * (m.static % 3))
            for f, n in steps(pe, F_TILES, 2, 3, N_FF, peel=1):
                if f.i is None and f.static == 0:
                    pe.wait_ge(x1_ready, KC + 3)
                    unit(n, HH, HL, A, ready=xfl_ready, past=1)
                    pe.wait_ge(fsq_added, KC + 1)
                    mm(Q[:, 2, 0:256], ones[:], facc[:, 0:256], start=True, stop=True)
                    mm(Q[:, 3, 0:264], ones[:], facc[:, 256:T], start=True, stop=True).then_inc(fsq_summed, 1)
                else:
                    pe.wait_ge(ffa_ready, f.val(1, 1))
                    unit(n, HH, HL, A)
                pe.wait_ge(ffb_ready, f.val(1, 1))
                unit(n.plus(1), HH, HL, B)
            pe.wait_ge(ffa_ready, F_TILES + 1)
            for m, n in steps(pe, KC, 3, 2, N_DOWN, loops=3, peel=2):
                if m.static != 0:
                    pe.wait_ge(x2_ready, m.val(1, 1))
                for j in range(3):
                    if m.static == 0:
                        pe.wait_ge(hidl_ready, DOWN_CUT[j + 1] + 1)
                    unit(n.plus(j), HIDH, HIDL, A if m.static % 2 == 0 else B, cols=range(DOWN_CUT[j], DOWN_CUT[j + 1]),
                         start=j == 0, stop=j == 2)
            pe.wait_ge(x2_added, KC + 1)
            mm(Q[:, 2, 0:256], ones[:], facc[:, 0:256], start=True, stop=True)
            mm(Q[:, 3, 0:264], ones[:], facc[:, 256:T], start=True, stop=True).then_inc(fsq_summed, 1)


def kernel(**inputs):
    import numpy as np
    import concourse.bacc as bacc
    from concourse.bass_utils import run_bass_kernel_spmd

    a = {k: np.asarray(v) for k, v in inputs.items()}
    f32 = np.float32

    def chunks(w, cols):
        return w[:, cols].reshape(-1, P, len(cols)).transpose(1, 0, 2)

    w_in, b_in = a["w_in"][0], a["b_in"][0]
    w_a, w_glu, w_b, w_out = a["w_a"][0], a["w_glu"][0], a["w_b"][0], a["w_out"][0]
    w1, w3, w2 = a["w_ff1"][0], a["w_ff3"][0], a["w_ff2"][0]
    OFF_G, OFF_U = 4 * D, 4 * D + 2 * H
    OFF_GA = OFF_U + 512
    OFF_GB = OFF_GA + D
    wst = np.zeros((N_UNITS, P, U), f32)
    tile = lambda off, m: np.arange(off + P * m, off + P * m + P)
    gates = wst[N_GATES].reshape(P, KC, P)
    gates[:, :, 0:H] = chunks(w_in, np.arange(OFF_G, OFF_G + H))
    gates[:, :, 32:32 + H] = chunks(w_in, np.arange(OFF_G + H, OFF_G + 2 * H))
    for h in range(H):
        n = N_MIX + PER_HEAD * h
        wst[n] = chunks(w_in, tile(OFF_U, h)).reshape(P, U)
        for e in range(NE):
            wst[n + 1 + e] = chunks(w_in, tile(D, NE * h + e)).reshape(P, U)
            wst[n + 3 + e] = chunks(w_in, tile(0, NE * h + e)).reshape(P, U)
            wst[n + 7 + e] = chunks(w_in, tile(3 * D, NE * h + e)).reshape(P, U)
        v = chunks(w_in, np.arange(2 * D + DH * h, 2 * D + DH * h + DH))
        wst[n + 5] = v[:, 0:4].reshape(P, U)
        wst[n + 6] = v[:, 4:8].reshape(P, U)
    for m in range(4):
        wst[N_GLU + m // 2][:, 512 * (m % 2):512 * (m % 2) + 512] = chunks(w_glu, tile(0, m)).reshape(P, 512)
    for m in range(KC):
        n = N_MERGE + PER_MERGE * m
        wst[n] = chunks(w_in, tile(OFF_GB, m)).reshape(P, U)
        wst[n + 1][:, 0:512] = chunks(w_b, tile(0, m)).reshape(P, 512)
        wst[n + 2] = chunks(w_in, tile(OFF_GA, m)).reshape(P, U)
        wst[n + 3] = chunks(w_a, tile(0, m)).reshape(P, U)
        wst[N_OUT + m] = chunks(w_out, tile(0, m)).reshape(P, U)
        down = chunks(w2, tile(0, m))
        for j in range(3):
            part = down[:, DOWN_CUT[j]:DOWN_CUT[j + 1]]
            wst[N_DOWN + 3 * m + j][:, 0:P * part.shape[1]] = part.reshape(P, -1)
    for f in range(F_TILES):
        wst[N_FF + 2 * f] = chunks(w1, tile(0, f)).reshape(P, U)
        wst[N_FF + 2 * f + 1] = chunks(w3, tile(0, f)).reshape(P, U)

    x = np.concatenate([a["x_prompt"].reshape(SEQ, D), a["x_sample"].reshape(NS, D)], axis=0)
    xt = np.ascontiguousarray(x.T.reshape(KC, P, T).transpose(1, 0, 2))

    col = lambda v: v.reshape(-1, P).T
    def s5_rows(g):
        c = np.broadcast_to(g.reshape(4, 8, 1, 64), (4, 8, 16, 64)).transpose(1, 2, 0, 3).reshape(P, 256)
        s = g.reshape(16, 2, 64).transpose(1, 2, 0).reshape(P, 16)
        return np.concatenate([c, s], axis=1)

    ldt = np.broadcast_to(a["s5_log_dt"][0][:, None], (32, 64))
    apar = np.ascontiguousarray(np.stack([s5_rows(a["s5_A_re"][0]), s5_rows(a["s5_A_im"][0]), s5_rows(ldt)], axis=1))

    def state_major(b):
        o = np.zeros((2, 64, 16, 2, 16), f32)
        v = b.reshape(16, 2, 64, 16)
        for g in range(2):
            o[g, :, :, g, :] = v[:, g].transpose(1, 0, 2)
        return o.reshape(P, 512)

    def channel_major(b):
        o = np.zeros((8, 16, 4, 2, 64), f32)
        v = b.reshape(4, 8, 64, 16)
        for g in range(8):
            o[g, :, :, g % 2, :] = v[:, g].transpose(2, 0, 1)
        return o.reshape(P, 512)

    small = np.zeros((P, NSM + 44), f32)

    def put(name, v, rows=slice(0, P)):
        small[rows, SM[name][0]:SM[name][1]] = v

    for part in ("re", "im"):
        bmat = a["s5_B_" + part][0]
        put("b_" + part, np.concatenate([channel_major(bmat), state_major(bmat)], axis=1))
        put("c_" + part, state_major(a["s5_C_" + part][0].transpose(0, 2, 1)))
    s0 = np.stack([a["state_s5_re"][0], a["state_s5_im"][0]])
    put("s0", s0.reshape(2, NS, 16, 2, 64).transpose(3, 4, 0, 2, 1).reshape(P, 256))
    put("n0", a["state_mlstm_n"][0].reshape(NS, H, NE, P).transpose(3, 1, 2, 0).reshape(P, 64))
    put("ident", np.eye(P, dtype=f32))
    put("m0", a["state_mlstm_m"][0].T, slice(0, H))
    small[0:H, SM["b_gate"][0]] = b_in[OFF_G:OFF_G + H]
    small[32:32 + H, SM["b_gate"][0] + 1] = b_in[OFF_G + H:OFF_G + 2 * H]
    hpar = np.zeros((P, H, 10), f32)
    bu, bq, bk, bo = col(b_in[OFF_U:OFF_GA]), col(b_in[0:D]), col(b_in[D:2 * D]), col(b_in[3 * D:4 * D])
    hpar[:, :, 0] = bu
    for e in range(NE):
        hpar[:, :, 1 + e], hpar[:, :, 3 + e], hpar[:, :, 5 + e] = bk[:, e::2], bq[:, e::2], bo[:, e::2]
        hpar[:, :, 8 + e] = col(a["mlstm_norm_g"][0])[:, e::2]
    hpar[:, :, 7] = col(a["s5_D"][0])
    put("hp", hpar.reshape(P, 40))
    small[:, NSM:NSM + 8] = col(a["norm_mix_g"][0])
    small[:, NSM + 8:NSM + 16] = col(a["norm_ffn_g"][0])
    small[:, NSM + 16:NSM + 24] = col(a["norm_final_g"])
    small[:, NSM + 24:NSM + 40:2] = col(b_in[OFF_GB:])
    small[:, NSM + 25:NSM + 40:2] = col(b_in[OFF_GA:OFF_GB])
    small[:, NSM + 40:NSM + 44] = col(a["b_glu"][0])
    vbias = np.ascontiguousarray(b_in[2 * D:3 * D].reshape(H, DH))
    c0 = np.ascontiguousarray(a["state_mlstm_C"][0].reshape(NS, H, NE, P, DH).transpose(1, 3, 0, 2, 4).reshape(H, P, NS * NE * DH))

    arrays = {"wst": wst, "xt": xt, "small": small, "apar": apar, "vbias": vbias, "c0": c0}
    outs = {"y": (P, KC, T), "cp": (H, P, NE * (DH + 1)), "mp": (H, 1), "s5p": (P, 2, 16),
            "cs": (H, P, NS * NE * DH), "ns": (P, H, NE, NS), "ms": (H, NS), "s5s": (P, 2, 16, NS)}
    nc = bacc.Bacc("TRN2", target_bir_lowering=False, num_devices=1)
    args = [nc.dram_tensor(k, v.shape, F32, kind="ExternalInput").ap() for k, v in arrays.items()]
    args += [nc.dram_tensor("out_" + k, s, F32, kind="ExternalOutput").ap() for k, s in outs.items()]
    build(nc, *args)
    res = run_bass_kernel_spmd(nc, [arrays], core_ids=[0]).results[0]
    r = {k: res["out_" + k] for k in outs}
    y = r["y"].transpose(1, 0, 2).reshape(D, T).T
    cp = r["cp"].reshape(H, P, NE, DH + 1).transpose(0, 2, 1, 3).reshape(H, DH, DH + 1)
    sp = r["s5p"].reshape(2, 64, 2, 16).transpose(2, 3, 0, 1).reshape(2, 1, 1, 32, 64)
    ss = r["s5s"].reshape(2, 64, 2, 16, NS).transpose(2, 4, 3, 0, 1).reshape(2, 1, NS, 32, 64)
    cs = r["cs"].reshape(H, P, NS, NE, DH).transpose(2, 0, 3, 1, 4).reshape(1, NS, H, DH, DH)
    ns = r["ns"].transpose(3, 1, 2, 0).reshape(1, NS, H, DH)
    c = np.ascontiguousarray
    return (c(y[:SEQ]).reshape(1, SEQ, D), c(y[SEQ:]).reshape(NS, 1, D),
            c(cp[:, :, :DH])[None, None], c(cp[:, :, DH])[None, None], c(r["mp"].reshape(1, 1, H)),
            c(sp[0]), c(sp[1]), c(cs), c(ns), c(r["ms"].T)[None], c(ss[0]), c(ss[1]))
```
